# Optimizing a Trainium2 kernel written in Bass

```python
import jax, jax.numpy as jnp
from jax import lax
import numpy as np

D_MODEL = 1024
BATCH = 1
SEQ = 1024
DEPTH = 1
DEC_BATCH = 8
DEC_SEQ = 1
PAST_LEN = 4096
PAGE_SIZE = 128

MIX_WIDTH = 2 * D_MODEL
GROUP_WIDTH = MIX_WIDTH // 4
POOL_WINDOWS = (2, 4, 8, 16)
POOL_GC = GROUP_WIDTH // len(POOL_WINDOWS)
POOL_BUF = max(POOL_WINDOWS) - 1
ML_HEADS = 4
ML_DK = GROUP_WIDTH // ML_HEADS
ML_DV = GROUP_WIDTH // ML_HEADS
ML_CHUNK = 128
SB_HEADS = 8
SB_DIM = GROUP_WIDTH // SB_HEADS
SB_BLOCK = 128
N_MEM = 256
MEM_HEADS = 4
MEM_DIM = GROUP_WIDTH // MEM_HEADS
EPS = 1e-6
IN_SPLITS = (GROUP_WIDTH, GROUP_WIDTH,
             GROUP_WIDTH, GROUP_WIDTH, GROUP_WIDTH, ML_HEADS, ML_HEADS, GROUP_WIDTH, GROUP_WIDTH,
             GROUP_WIDTH, GROUP_WIDTH, GROUP_WIDTH, GROUP_WIDTH,
             GROUP_WIDTH, GROUP_WIDTH)
IN_COLS = sum(IN_SPLITS)
SPLIT_POINTS = tuple(int(s) for s in np.cumsum(IN_SPLITS)[:-1])

kernel_name = "hymba_pool_mlstm_stickbreak_memxattn_step"

def rms_norm(x, g):
    xf = x.astype(jnp.float32)
    y = xf * lax.rsqrt(jnp.mean(xf * xf, axis=-1, keepdims=True) + EPS)
    return (y * g.astype(jnp.float32)).astype(x.dtype)

def pool_mix(u, buf, pos0, pool_w, pool_scale):
    B, T, C = u.shape
    P = POOL_BUF
    ext = jnp.concatenate([buf.astype(u.dtype), u], axis=1).astype(jnp.float32)
    cs = jnp.concatenate([jnp.zeros((B, 1, C), jnp.float32), jnp.cumsum(ext, axis=1)], axis=1)
    pos = pos0 + jnp.arange(T)
    cur = ext[:, P:]
    outs = []
    for g, w in enumerate(POOL_WINDOWS):
        sl = slice(g * POOL_GC, (g + 1) * POOL_GC)
        s = cs[:, P + 1:P + 1 + T, sl] - cs[:, P + 1 - w:P + 1 - w + T, sl]
        cnt = jnp.minimum(pos + 1, w).astype(jnp.float32)[None, :, None]
        outs.append(s / cnt - cur[..., sl])
    pooled = jnp.stack(outs, axis=2)
    y = jnp.einsum('btgc,gcd->btgd', pooled, pool_w.astype(jnp.float32)).reshape(B, T, C)
    y = y * pool_scale.astype(jnp.float32)
    new_buf = ext[:, -P:].astype(u.dtype)
    return y.astype(u.dtype), new_buf

def mlstm(q, k, v, i_pre, logf, C0, n0, m0):
    B, T, H, DK = q.shape
    DV = v.shape[-1]
    L = ML_CHUNK if T % ML_CHUNK == 0 else T
    nc = T // L
    f32 = jnp.float32

    def chunks(a):
        return jnp.moveaxis(a.astype(f32).reshape((B, nc, L) + a.shape[2:]), 1, 0)

    xs = (chunks(q), chunks(k.astype(f32) * DK ** -0.5), chunks(v), chunks(i_pre), chunks(logf))
    causal = jnp.tril(jnp.ones((L, L), dtype=bool))

    def step(carry, inp):
        C, n, m = carry
        qc, kc, vc, ic, fc = inp
        b = jnp.cumsum(fc, axis=1).transpose(0, 2, 1)
        ih = ic.transpose(0, 2, 1)
        D = jnp.where(causal, b[..., :, None] - b[..., None, :] + ih[..., None, :], -jnp.inf)
        inter = b + m[..., None]
        m_t = jnp.maximum(inter, jnp.max(D, axis=-1))
        w_intra = jnp.exp(D - m_t[..., None])
        w_inter = jnp.exp(inter - m_t)
        S = jnp.einsum('bthd,bshd->bhts', qc, kc) * w_intra
        num = (jnp.einsum('bhts,bshv->bthv', S, vc)
               + jnp.einsum('bthd,bhdv->bthv', qc, C) * w_inter.transpose(0, 2, 1)[..., None])
        den = jnp.sum(S, axis=-1) + w_inter * jnp.einsum('bthd,bhd->bht', qc, n)
        hc = num / jnp.maximum(jnp.abs(den), jnp.exp(-m_t)).transpose(0, 2, 1)[..., None]
        bL = b[..., -1]
        g = bL[..., None] - b + ih
        m_new = jnp.maximum(bL + m, jnp.max(g, axis=-1))
        w_old = jnp.exp(bL + m - m_new)
        w_s = jnp.exp(g - m_new[..., None])
        C_new = w_old[..., None, None] * C + jnp.einsum('bhs,bshd,bshv->bhdv', w_s, kc, vc)
        n_new = w_old[..., None] * n + jnp.einsum('bhs,bshd->bhd', w_s, kc)
        return (C_new, n_new, m_new), hc

    (C, n, m), hs = lax.scan(step, (C0.astype(f32), n0.astype(f32), m0.astype(f32)), xs)
    h = jnp.moveaxis(hs, 0, 1).reshape(B, T, H, DV)
    return h, C, n, m

def stick_breaking(q, k, v, q_off, logit_bias):
    B, T, H, Dh = q.shape
    S = k.shape[1]
    BQ = SB_BLOCK if T % SB_BLOCK == 0 else T
    nb = T // BQ
    f32 = jnp.float32
    kf = k.astype(f32)
    vf = v.astype(f32)
    bias = logit_bias.astype(f32)[None, :, None, None]
    kpos = jnp.arange(S)
    qb = jnp.moveaxis(q.astype(f32).reshape(B, nb, BQ, H, Dh), 1, 0)
    qpos = (q_off + jnp.arange(T)).reshape(nb, BQ)

    def block(inp):
        qi, pi = inp
        z = jnp.einsum('bqhd,bshd->bhqs', qi, kf) * Dh ** -0.5 + bias
        mask = kpos[None, :] < pi[:, None]
        l1mb = jnp.where(mask, jax.nn.log_sigmoid(-z), 0.0)
        after = lax.cumsum(l1mb, axis=3, reverse=True) - l1mb
        A = jnp.where(mask, jnp.exp(jax.nn.log_sigmoid(z) + after), 0.0)
        return jnp.einsum('bhqs,bshd->bqhd', A, vf)

    out = lax.map(block, (qb, qpos))
    return jnp.moveaxis(out, 0, 1).reshape(B, T, H, Dh).astype(q.dtype)

def mem_attention(q, mk, mv):
    s = jnp.einsum('bthd,bmhd->bhtm', q.astype(jnp.float32), mk.astype(jnp.float32)) * MEM_DIM ** -0.5
    p = jax.nn.softmax(s, axis=-1)
    return jnp.einsum('bhtm,bmhd->bthd', p, mv.astype(jnp.float32)).astype(q.dtype)

def mem_kv(mem, mem_norm, w_mem_kv):
    B = mem.shape[0]
    kv = jnp.einsum('bmd,dc->bmc', rms_norm(mem, mem_norm), w_mem_kv)
    mk, mv = jnp.split(kv, 2, axis=-1)
    return mk.reshape(B, N_MEM, MEM_HEADS, MEM_DIM), mv.reshape(B, N_MEM, MEM_HEADS, MEM_DIM)

def layer(x, mem_k, mem_v, pool_buf, C0, n0, m0, k_past, v_past,
          norm_pre, norm_post, w_in, pool_w, pool_scale, gate_bias, ml_norm, sb_bias, w_out):
    B, T, _ = x.shape
    pos0 = k_past.shape[1]
    h = rms_norm(x, norm_pre)
    proj = jnp.einsum('btd,dc->btc', h, w_in)
    (a_u, a_g, b_q, b_k, b_v, b_i, b_f, b_o, b_g,
     c_q, c_k, c_v, c_g, d_q, d_g) = jnp.split(proj, SPLIT_POINTS, axis=-1)

    ya, new_buf = pool_mix(a_u, pool_buf, pos0, pool_w, pool_scale)
    ya = ya * jax.nn.silu(a_g)

    i_pre = (b_i + gate_bias[0]).astype(jnp.float32)
    logf = jax.nn.log_sigmoid((b_f + gate_bias[1]).astype(jnp.float32))
    hb, C, n, m = mlstm(b_q.reshape(B, T, ML_HEADS, ML_DK), b_k.reshape(B, T, ML_HEADS, ML_DK),
                        b_v.reshape(B, T, ML_HEADS, ML_DV), i_pre, logf, C0, n0, m0)
    hb = (jax.nn.sigmoid(b_o.astype(jnp.float32)).reshape(B, T, ML_HEADS, ML_DV) * hb).astype(x.dtype)
    hb = rms_norm(hb, ml_norm.reshape(ML_HEADS, ML_DV)).reshape(B, T, GROUP_WIDTH)
    yb = hb * jax.nn.silu(b_g)

    kc = c_k.reshape(B, T, SB_HEADS, SB_DIM)
    vc = c_v.reshape(B, T, SB_HEADS, SB_DIM)
    k_all = jnp.concatenate([k_past.astype(kc.dtype), kc], axis=1)
    v_all = jnp.concatenate([v_past.astype(vc.dtype), vc], axis=1)
    yc = stick_breaking(c_q.reshape(B, T, SB_HEADS, SB_DIM), k_all, v_all, pos0, sb_bias)
    yc = yc.reshape(B, T, GROUP_WIDTH) * jax.nn.silu(c_g)

    yd = mem_attention(d_q.reshape(B, T, MEM_HEADS, MEM_DIM), mem_k, mem_v).reshape(B, T, GROUP_WIDTH)
    yd = yd * jax.nn.silu(d_g)

    mix = jnp.concatenate([ya, yb, yc, yd], axis=-1)
    out = rms_norm(jnp.einsum('btc,cd->btd', mix, w_out), norm_post)
    st = (new_buf, C.astype(x.dtype), n.astype(x.dtype), m.astype(x.dtype), kc, vc)
    return x + out, st

def setup_inputs(seed: int = 0) -> dict:
    key = jax.random.key(seed)
    ks = jax.random.split(key, 24)
    f32 = jnp.float32
    n_pages = PAST_LEN // PAGE_SIZE
    n_used = DEC_BATCH * n_pages
    n_phys = (n_used * 5) // 4
    nrm = lambda k, shape, s=1.0: jax.random.normal(k, shape, f32) * s
    page_table = jax.random.permutation(ks[0], n_phys)[:n_used].reshape(DEC_BATCH, n_pages).astype(jnp.int32)
    gate_bias = jnp.stack([nrm(ks[20], (DEPTH, ML_HEADS), 0.1),
                           3.0 + nrm(ks[21], (DEPTH, ML_HEADS), 0.1)], axis=1)
    sb_bias = -4.0 - 4.0 * jax.random.uniform(ks[23], (DEPTH, SB_HEADS), f32)
    return {
        "x_prompt": nrm(ks[1], (BATCH, SEQ, D_MODEL)),
        "x_sample": nrm(ks[2], (DEC_BATCH, DEC_SEQ, D_MODEL)),
        "mem_prompt": nrm(ks[3], (BATCH, N_MEM, D_MODEL)),
        "state_pool_buf": nrm(ks[4], (DEPTH, DEC_BATCH, POOL_BUF, GROUP_WIDTH)),
        "state_mlstm_C": nrm(ks[5], (DEPTH, DEC_BATCH, ML_HEADS, ML_DK, ML_DV), 0.5),
        "state_mlstm_n": nrm(ks[6], (DEPTH, DEC_BATCH, ML_HEADS, ML_DK), 0.5),
        "state_mlstm_m": nrm(ks[7], (DEPTH, DEC_BATCH, ML_HEADS)),
        "cache_sb_k": nrm(ks[8], (DEPTH, n_phys, PAGE_SIZE, SB_HEADS, SB_DIM)),
        "cache_sb_v": nrm(ks[9], (DEPTH, n_phys, PAGE_SIZE, SB_HEADS, SB_DIM)),
        "cache_mem_k": nrm(ks[10], (DEPTH, DEC_BATCH, N_MEM, MEM_HEADS, MEM_DIM)),
        "cache_mem_v": nrm(ks[11], (DEPTH, DEC_BATCH, N_MEM, MEM_HEADS, MEM_DIM)),
        "page_table": page_table,
        "norm_pre": 1.0 + nrm(ks[12], (DEPTH, D_MODEL), 0.05),
        "norm_post": 1.0 + nrm(ks[13], (DEPTH, D_MODEL), 0.05),
        "w_in": nrm(ks[14], (DEPTH, D_MODEL, IN_COLS), D_MODEL ** -0.5),
        "pool_w": nrm(ks[15], (DEPTH, len(POOL_WINDOWS), POOL_GC, POOL_GC), POOL_GC ** -0.5),
        "pool_scale": 1.0 + nrm(ks[16], (DEPTH, GROUP_WIDTH), 0.1),
        "mlstm_gate_bias": gate_bias,
        "mlstm_norm": 1.0 + nrm(ks[17], (DEPTH, GROUP_WIDTH), 0.05),
        "sb_logit_bias": sb_bias,
        "mem_norm": 1.0 + nrm(ks[18], (DEPTH, D_MODEL), 0.05),
        "w_mem_kv": nrm(ks[19], (DEPTH, D_MODEL, 2 * GROUP_WIDTH), D_MODEL ** -0.5),
        "w_out": nrm(ks[22], (DEPTH, MIX_WIDTH, D_MODEL), MIX_WIDTH ** -0.5),
    }

def reference(x_prompt, x_sample, mem_prompt, state_pool_buf, state_mlstm_C, state_mlstm_n,
              state_mlstm_m, cache_sb_k, cache_sb_v, cache_mem_k, cache_mem_v, page_table,
              norm_pre, norm_post, w_in, pool_w, pool_scale, mlstm_gate_bias, mlstm_norm,
              sb_logit_bias, mem_norm, w_mem_kv, w_out):
    B = x_prompt.shape[0]
    DB = x_sample.shape[0]
    n_pages = page_table.shape[1]
    past = n_pages * PAGE_SIZE
    dt = x_prompt.dtype
    yp, ys = x_prompt, x_sample
    pb_p, pb_s, C_p, C_s, n_p, n_s, m_p, m_s = [], [], [], [], [], [], [], []
    k_p, k_s, v_p, v_s, mk_out, mv_out = [], [], [], [], [], []
    for l in range(DEPTH):
        w = (norm_pre[l], norm_post[l], w_in[l], pool_w[l], pool_scale[l],
             mlstm_gate_bias[l], mlstm_norm[l], sb_logit_bias[l], w_out[l])
        mk, mv = mem_kv(mem_prompt, mem_norm[l], w_mem_kv[l])
        yp, st = layer(yp, mk, mv,
                       jnp.zeros((B, POOL_BUF, GROUP_WIDTH), dt),
                       jnp.zeros((B, ML_HEADS, ML_DK, ML_DV), jnp.float32),
                       jnp.zeros((B, ML_HEADS, ML_DK), jnp.float32),
                       jnp.zeros((B, ML_HEADS), jnp.float32),
                       jnp.zeros((B, 0, SB_HEADS, SB_DIM), dt),
                       jnp.zeros((B, 0, SB_HEADS, SB_DIM), dt), *w)
        pb_p.append(st[0]); C_p.append(st[1]); n_p.append(st[2]); m_p.append(st[3])
        k_p.append(st[4]); v_p.append(st[5]); mk_out.append(mk); mv_out.append(mv)
        k_past = cache_sb_k[l][page_table].reshape(DB, past, SB_HEADS, SB_DIM)
        v_past = cache_sb_v[l][page_table].reshape(DB, past, SB_HEADS, SB_DIM)
        ys, st = layer(ys, cache_mem_k[l], cache_mem_v[l], state_pool_buf[l], state_mlstm_C[l],
                       state_mlstm_n[l], state_mlstm_m[l], k_past, v_past, *w)
        pb_s.append(st[0]); C_s.append(st[1]); n_s.append(st[2]); m_s.append(st[3])
        k_s.append(st[4]); v_s.append(st[5])
    return (yp, ys,
            jnp.stack(pb_p), jnp.stack(pb_s),
            jnp.stack(C_p), jnp.stack(C_s),
            jnp.stack(n_p), jnp.stack(n_s),
            jnp.stack(m_p), jnp.stack(m_s),
            jnp.stack(k_p), jnp.stack(k_s),
            jnp.stack(v_p), jnp.stack(v_s),
            jnp.stack(mk_out), jnp.stack(mv_out))


_drawn_inputs = setup_inputs


def setup_inputs(seed=0):
    import zlib

    import numpy as np

    out = dict(_drawn_inputs(seed))
    spreads = {}
    factors = {}
    for name, (base, spread) in spreads.items():
        noise = np.random.default_rng([zlib.crc32(name.encode()), seed]).standard_normal(out[name].shape)
        drawn = base * np.exp(spread * noise) if base else spread * noise
        out[name] = __import__('jax').numpy.asarray(drawn.astype(out[name].dtype))
    for name, factor in factors.items():
        out[name] = (out[name] * factor).astype(out[name].dtype)
    return out
```

```python
from contextlib import ExitStack, contextmanager

import concourse.bass as bass
from concourse import mybir

ALU = mybir.AluOpType
ACT = mybir.ActivationFunctionType
AXX = mybir.AxisListType.X
F32 = mybir.dt.float32
F32R = mybir.dt.float32r
I32 = mybir.dt.int32

P = 128
DM = 1024
KT = DM // P
T = 1024
NB = 8
NT = T + NB
CH = NT // 3
GW = 512
GT = GW // P
TB = T // P
PAST = 4096
PAGE = 128
NPG = PAST // PAGE
SBH, SBD = 8, 64
SCORE_SCALE = SBD ** -0.5
MLH, DK = 4, 128
NMEM = 256
POOL_BUF = 15
EPS = 1e-6
LN_EXP = 6
FAR = -30000.0
BIG = 3.0e38

A_U, A_G = 0, GW
B_Q, B_K, B_V = 2 * GW, 3 * GW, 4 * GW
B_IF = 5 * GW
B_O, B_G = B_IF + 2 * MLH, B_IF + 2 * MLH + GW
C_Q, C_K, C_V, C_G = (B_G + GW * n for n in range(1, 5))
D_Q, D_G = C_G + GW, C_G + 2 * GW


@contextmanager
def stage(nc):
    before = nc.snapshot_sems()
    with ExitStack() as ctx:
        yield ctx
    nc.clear_and_free_semaphores(nc.allocated_since(before))
    nc.all_engine_barrier()


class Signal:

    def __init__(self, ctx, nc, name, per, unit=1):
        self.sem = nc.alloc_semaphore(name)
        self.per, self.unit = per, unit

    def credit(self, engine):
        engine.sem_inc(self.sem, self.per * self.unit)

    def at(self, i, n):
        passes = i + 1 if self.unit == 1 else i
        return passes * (self.per * self.unit) + n * self.unit


def store_mix(nc, pool, k, tile, mix, mix_out, i, mix_free):
    pool.sem_inc(mix_free.sem, 1)
    pool.dma_start(k.mix_dram[bass.ds(tile, 1)].rearrange("a p t -> p (a t)"), mix[:, 0:T]).then_inc(mix_out.sem, 16)
    pool.wait_ge(mix_out.sem, mix_out.at(i, 1))
    pool.sem_inc(mix_free.sem, 1)


def load_tables(nc, act, which):
    act.add_instruction(mybir.InstLoadActFuncSet(name=nc.get_next_instruction_name(),
                                                 act_func_set_id=which, ins=[], outs=[]))


def normalise_and_transpose(nc, ctx, tag, row_tiles, gain, xh, xl, ident, eps, psum):
    sb = lambda name, shape, dt=F32: ctx.enter_context(nc.sbuf_tensor(f"{tag}_{name}", shape, dt))
    sem = lambda name: nc.alloc_semaphore(f"{tag}_{name}")
    n_tiles = len(row_tiles)
    rows = sb("rows", [P, 2, DM])
    squares = sb("squares", [P, DM])
    normed = sb("normed", [P, 2, DM])
    gain_b = sb("gain_b", [P, DM])
    stat = sb("stat", [P, 3, n_tiles])
    gain_in = sem("gain_in")
    rows_in = [sem("rows_in0"), sem("rows_in1")]
    sum_done, ln_done, rstd_done = sem("sum_done"), sem("ln_done"), sem("rstd_done")
    normed_done, turned, hi_done, lo_done = sem("normed_done"), sem("turned"), sem("hi_done"), sem("lo_done")

    with nc.Block() as block:

        @block.sync
        def _(sp):
            sp.dma_start(gain_b[:], gain.to_broadcast([P, DM])).then_inc(gain_in, 16)
            for r, (src, n, _) in enumerate(row_tiles):
                if r >= 2:
                    sp.wait_ge(normed_done, r - 1)
                sp.dma_start(rows[0:n, r % 2, :], src).then_inc(rows_in[r % 2], 16)

        @block.scalar
        def _(act):
            def statistics(r):
                n = row_tiles[r][1]
                act.wait_ge(rows_in[r % 2], 16 * (r // 2 + 1))
                if r:
                    act.wait_ge(sum_done, r)
                nc.scalar.activation(squares[0:n, :], rows[0:n, r % 2, :], ACT.Square,
                                     accum_out=stat[0:n, 0, r:r + 1]).then_inc(sum_done, 1)
                act.wait_ge(sum_done, r + 1)
                nc.scalar.activation(stat[0:n, 1, r:r + 1], stat[0:n, 0, r:r + 1], ACT.Ln,
                                     scale=1.0 / DM, bias=eps[0:n, :]).then_inc(ln_done, 1)
                act.wait_ge(ln_done, r + 1)
                nc.scalar.activation(stat[0:n, 2, r:r + 1], stat[0:n, 1, r:r + 1], ACT.Exp,
                                     scale=-0.5).then_inc(rstd_done, 1)

            def high_part(r):
                _, n, c0 = row_tiles[r]
                for q in range(2):
                    act.wait_ge(turned, 2 * r + q + 1)
                    nc.scalar.activation(xh[:, 4 * q:4 * q + 4, c0:c0 + n], psum[(2 * r + q) % 4][:, :, 0:n],
                                         ACT.Copy).then_inc(hi_done, 1)

            load_tables(nc, act, LN_EXP)
            statistics(0)
            for r in range(n_tiles):
                if r + 1 < n_tiles:
                    statistics(r + 1)
                high_part(r)

        @block.vector
        def _(dve):
            def normalise(r):
                n = row_tiles[r][1]
                dve.wait_ge(rstd_done, r + 1)
                if r == 0:
                    dve.wait_ge(gain_in, 16)
                if r >= 2:
                    dve.wait_ge(turned, 2 * r - 2)
                nc.vector.scalar_tensor_tensor(out=normed[0:n, r % 2, :], in0=rows[0:n, r % 2, :],
                                               scalar=stat[0:n, 2, r:r + 1], in1=gain_b[0:n, :],
                                               op0=ALU.mult, op1=ALU.mult).then_inc(normed_done, 1)

            def low_part(r):
                _, n, c0 = row_tiles[r]
                for q in range(2):
                    dve.wait_ge(hi_done, 2 * r + q + 1)
                    nc.vector.tensor_tensor(xl[:, 4 * q:4 * q + 4, c0:c0 + n], psum[(2 * r + q) % 4][:, :, 0:n],
                                            xh[:, 4 * q:4 * q + 4, c0:c0 + n].bitcast(F32),
                                            ALU.subtract).then_inc(lo_done, 1)

            normalise(0)
            for r in range(n_tiles):
                if r + 1 < n_tiles:
                    normalise(r + 1)
                low_part(r)

        @block.tensor
        def _(pe):
            for r, (_, n, _) in enumerate(row_tiles):
                pe.wait_ge(normed_done, r + 1)
                for q in range(2):
                    if r >= 2:
                        pe.wait_ge(lo_done, 2 * (r - 2) + q + 1)
                    for k in range(4 * q, 4 * q + 4):
                        last = nc.tensor.transpose(psum[(2 * r + q) % 4][:, k % 4, 0:n],
                                                   normed[0:n, r % 2, k * P:(k + 1) * P], ident[0:n, 0:n])
                    last.then_inc(turned, 1)


class Projection:

    def __init__(self, ctx, nc, tag, tiles, slots, xh, xl, banks, width=CH):
        sb = lambda name, dt: ctx.enter_context(nc.sbuf_tensor(f"{tag}_{name}", [P, slots, KT, P], dt))
        self.nc, self.tiles, self.slots, self.xh, self.xl, self.banks = nc, tiles, slots, xh, xl, banks
        self.chunks, self.width = len(banks), width
        self.raw, self.hi, self.lo = sb("w_raw", F32), sb("w_hi", F32R), sb("w_lo", F32R)
        uses = [len(range(s, tiles, slots)) for s in range(slots)]
        self.landed = [Signal(ctx, nc, f"{tag}_w_landed{s}", uses[s], 16) for s in range(slots)]
        self.hi_ready = Signal(ctx, nc, f"{tag}_w_hi_ready", tiles)
        self.lo_ready = Signal(ctx, nc, f"{tag}_w_lo_ready", tiles)
        self.projected = Signal(ctx, nc, f"{tag}_projected", self.chunks * tiles)
        self.taken = Signal(ctx, nc, f"{tag}_taken", self.chunks * tiles)

    def reach(self, j):
        s = j % self.slots
        earlier = [t for t in range(j) if t % self.slots == s] or \
                  [t - self.tiles for t in range(self.tiles) if t % self.slots == s]
        return j - earlier[-1]

    def load(self, sp, i, j, columns):
        prev = j - self.reach(j)
        sp.wait_ge(self.hi_ready.sem, self.hi_ready.at(i, prev + 1))
        sp.wait_ge(self.lo_ready.sem, self.lo_ready.at(i, prev + 1))
        sp.dma_start(self.raw[:, j % self.slots, :, :], columns).then_inc(self.landed[j % self.slots].sem, 16)

    def split_hi(self, act, i, j):
        s, prev = j % self.slots, j - self.reach(j)
        act.wait_ge(self.landed[s].sem, self.landed[s].at(i, j // self.slots + 1))
        act.wait_ge(self.projected.sem, self.projected.at(i, self.chunks * (prev + 1)))
        self.nc.scalar.activation(self.hi[:, s], self.raw[:, s], ACT.Copy).then_inc(self.hi_ready.sem, 1)

    def split_lo(self, dve, i, j):
        s = j % self.slots
        dve.wait_ge(self.hi_ready.sem, self.hi_ready.at(i, j + 1))
        self.nc.vector.tensor_tensor(self.lo[:, s], self.raw[:, s], self.hi[:, s].bitcast(F32),
                                     ALU.subtract).then_inc(self.lo_ready.sem, 1)

    def multiply(self, pe, i, j):
        s = j % self.slots
        pe.wait_ge(self.hi_ready.sem, self.hi_ready.at(i, j + 1))
        pe.wait_ge(self.lo_ready.sem, self.lo_ready.at(i, j + 1))
        for c in range(self.chunks):
            pe.wait_ge(self.taken.sem, self.taken.at(i, self.chunks * (j - 1) + c + 1))
            for k in range(KT):
                for n, (w, x) in enumerate(((self.hi, self.xh), (self.hi, self.xl), (self.lo, self.xh))):
                    last = self.nc.tensor.matmul(self.banks[c][:, 0:self.width], w[:, s, k, :],
                                                 x[:, k, c * self.width:(c + 1) * self.width],
                                                 start=(k == 0 and n == 0), stop=(k == KT - 1 and n == 2))
            last.then_inc(self.projected.sem, 1)

    def take(self, act, i, j, out, func, scale=1.0):
        for c in range(self.chunks):
            act.wait_ge(self.projected.sem, self.projected.at(i, self.chunks * j + c + 1))
            self.nc.scalar.activation(out(c), self.banks[c][:, 0:self.width], func,
                                      scale=scale).then_inc(self.taken.sem, 1)


def stick_breaking_prompt(nc, ctx, k):
    sb = lambda name, shape, dt=F32: ctx.enter_context(nc.sbuf_tensor(name, shape, dt))
    proj = Projection(ctx, nc, "c", 4, 2, k.xh, k.xl, k.bank[0:3])
    kT, qT, vT = sb("c_kT", [P, NT]), sb("c_qT", [P, NT]), sb("c_vT", [P, NT])
    k_tok, v_tok = sb("c_k_tok", [P, TB, P]), sb("c_v_tok", [P, TB, P])
    mix = sb("c_mix", [P, NT])
    new_tok = sb("c_new_tok", [NB, 2, P])
    bias_all, bias = sb("c_bias_all", [P, SBH]), sb("c_bias", [P, 2])
    W = 512
    z = sb("c_z", [P, 4, W])
    soft = sb("c_soft", [P, 2, W])
    L = sb("c_L", [P, 3, W])
    A = sb("c_A", [P, 3, W])
    later = sb("c_later", [P, 2, W])
    steps = [(c, j, h) for c in range(T // W) for j in reversed(range((c + 1) * W // P)) for h in range(2)]
    NS = len(steps)
    first_of_chunk = {(c, h): next(n for n, s in enumerate(steps) if s[0] == c and s[2] == h)
                      for c in range(T // W) for h in range(2)}
    col0 = lambda c, j: max(0, j * P - c * W)

    S = lambda name, per, unit=1: Signal(ctx, nc, "c_" + name, per, unit)
    bias_in, sending = (nc.alloc_semaphore(n) for n in ("c_bias_in", "c_sending"))
    bias_set = S("bias_set", 1)
    tok_turned, tok_taken = S("tok_turned", 5), S("tok_taken", 5)
    scores, z_ready = S("scores", NS), S("z_ready", NS)
    abs_done, exp_done, ln_done = S("abs_done", NS), S("exp_done", NS), S("ln_done", NS)
    L_ready, summed, x_ready, A_ready = S("L_ready", NS), S("summed", NS), S("x_ready", NS), S("A_ready", NS)
    weighted, later_ready = S("weighted", NS), S("later_ready", NS + 4)
    y_taken = S("y_taken", 2)
    written = S("written", 1)
    gate_kept, mix_out, mix_free = S("gate_kept", 1), S("mix_out", 1, 16), S("mix_free", 2)
    k_out, v_out, new_out = S("k_out", 1, 16), S("v_out", 1, 16), S("new_out", 2, 16)
    paged = PagedAttention(ctx, nc, k, "cp", 0, GT, 4, k.bank[0], k.bank[1], k.bank[2], k.bank[3])
    NP = paged.PAIRS
    FIRST_WEIGH = NS + 4 - NP
    Z, SUM, Y = k.bank[3:5], k.bank[5:7], k.bank[7]
    quad = lambda bank: bank[:, :].rearrange("p (b t) -> p b t", b=4)

    def later_count(n):
        return n + 1 + sum(first <= n for first in first_of_chunk.values())

    with nc.Block() as block:

        @block.sync
        def _(sp):
            sp.dma_start(bias_all[:], k.sb_logit_bias.to_broadcast([P, SBH])).then_inc(bias_in, 16)
            written.credit(sp)
            paged.setup_sync(sp)
            with sp.Fori(0, GT) as i:
                first = [sp.snap(i * P + base) for base in (C_V, C_K, C_Q, C_G)]
                paged.load_query(sp, i)
                for j in range(4):
                    proj.load(sp, i, j, k.w_in[:, :, bass.ds(first[j], P)])
                    for r in ((), range(0, 7), range(7, 10), range(10, NP))[j]:
                        paged.load_keys(sp, i, r)
                sp.wait_ge(tok_taken.sem, tok_taken.at(i, 2))
                sp.sem_inc(sending, 1)
                sp.dma_start(k.sb_v_prompt[:, :, bass.ds(i * P, P)], v_tok[:]).then_inc(v_out.sem, 16)
                sp.wait_ge(tok_taken.sem, tok_taken.at(i, 4))
                sp.sem_inc(sending, 1)
                sp.dma_start(k.sb_k_prompt[:, :, bass.ds(i * P, P)], k_tok[:]).then_inc(k_out.sem, 16)
                sp.wait_ge(tok_taken.sem, tok_taken.at(i, 5))
                sp.sem_inc(sending, 1)
                sp.dma_start(k.sb_k_sample[:, bass.ds(i * P, P)], new_tok[:, 0]).then_inc(new_out.sem, 16)
                sp.dma_start(k.sb_v_sample[:, bass.ds(i * P, P)], new_tok[:, 1]).then_inc(new_out.sem, 16)
                for s, n in ((k_out, 1), (v_out, 1), (new_out, 2)):
                    sp.wait_ge(s.sem, s.at(i, n))
                    sp.sem_inc(sending, 1)
                sp.sem_inc(written.sem, 1)
                paged.load_all_values(sp, i)

        @block.scalar
        def _(act):
            for s in (proj.hi_ready, proj.taken, abs_done, exp_done, ln_done, A_ready):
                s.credit(act)
            paged.setup_scalar(act)
            with act.Fori(0, GT) as i:
                chunk = lambda dst: lambda c: dst[:, c * CH:(c + 1) * CH]
                proj.split_hi(act, i, 0)
                proj.split_hi(act, i, 1)
                proj.take(act, i, 0, chunk(vT), ACT.Copy)
                proj.split_hi(act, i, 2)
                proj.take(act, i, 1, chunk(kT), ACT.Copy)
                proj.split_hi(act, i, 3)
                proj.take(act, i, 2, chunk(qT), ACT.Copy, scale=SCORE_SCALE)
                act.wait_ge(mix_free.sem, mix_free.at(i, 0))
                act.wait_ge(gate_kept.sem, gate_kept.at(i, 0))
                proj.take(act, i, 3, chunk(mix), ACT.Silu)

                load_tables(nc, act, LN_EXP)

                def softplus(n):
                    c, j, h = steps[n]
                    a = col0(c, j)
                    act.wait_ge(z_ready.sem, z_ready.at(i, n + 1))
                    act.wait_ge(L_ready.sem, L_ready.at(i, n - 1))
                    nc.scalar.activation(soft[:, n % 2, a:W], z[:, n % 4, a:W], ACT.Abs).then_inc(abs_done.sem, 1)
                    act.wait_ge(abs_done.sem, abs_done.at(i, n + 1))
                    nc.scalar.activation(soft[:, n % 2, a:W], soft[:, n % 2, a:W], ACT.Exp,
                                         scale=-1.0).then_inc(exp_done.sem, 1)
                    act.wait_ge(exp_done.sem, exp_done.at(i, n + 1))
                    nc.scalar.activation(soft[:, n % 2, a:W], soft[:, n % 2, a:W], ACT.Ln,
                                         bias=1.0).then_inc(ln_done.sem, 1)

                def weights(n):
                    c, j, h = steps[n]
                    a = col0(c, j)
                    act.wait_ge(x_ready.sem, x_ready.at(i, n + 1))
                    act.wait_ge(weighted.sem, weighted.at(i, n - 2))
                    nc.scalar.activation(A[:, n % 3, a:W], z[:, n % 4, a:W], ACT.Exp).then_inc(A_ready.sem, 1)

                for n in range(NS + 2):
                    if n < NS:
                        softplus(n)
                    if n >= 2:
                        weights(n - 2)
                    if n == 6:
                        paged.softplus_tail(act, i)
                    if n == 10:
                        paged.weights(act, i)

        @block.vector
        def _(dve):
            dve.wait_ge(bias_in, 16)
            paged.setup_vector(dve)
            for s in (proj.lo_ready, bias_set, tok_taken, z_ready, L_ready, x_ready, y_taken, gate_kept):
                s.credit(dve)
            with dve.Fori(0, GT) as i:
                proj.split_lo(dve, i, 0)
                proj.split_lo(dve, i, 1)
                for r in range(4):
                    paged.reduce_keys(dve, i, r)
                proj.split_lo(dve, i, 2)
                nc.vector.tensor_copy(bias[:], bias_all[:, bass.ds(i * 2, 2)]).then_inc(bias_set.sem, 1)
                for r in range(4, 7):
                    paged.reduce_keys(dve, i, r)
                dve.wait_ge(written.sem, written.at(i, 0))
                for q in range(2):
                    dve.wait_ge(tok_turned.sem, tok_turned.at(i, q + 1))
                    nc.vector.tensor_copy(v_tok[:, 4 * q:4 * q + 4, :], quad(SUM[q])).then_inc(tok_taken.sem, 1)
                proj.split_lo(dve, i, 3)
                for r in range(7, 11):
                    paged.reduce_keys(dve, i, r)
                for q in range(2):
                    dve.wait_ge(tok_turned.sem, tok_turned.at(i, q + 3))
                    nc.vector.tensor_copy(k_tok[:, 4 * q:4 * q + 4, :], quad(Z[q])).then_inc(tok_taken.sem, 1)
                dve.wait_ge(tok_turned.sem, tok_turned.at(i, 5))
                nc.vector.tensor_copy(new_tok[:].rearrange("p a b -> p (a b)"), Y[0:NB, 0:2 * P]).then_inc(tok_taken.sem, 1)
                for r in range(11, 14):
                    paged.reduce_keys(dve, i, r)
                dve.wait_ge(proj.taken.sem, proj.taken.at(i, 12))
                nc.vector.tensor_copy(k.new_mix[:, bass.ds(i + 2 * GT, 1), :].rearrange("p a b -> p (a b)"),
                                      mix[:, T:NT]).then_inc(gate_kept.sem, 1)
                dve.wait_ge(bias_set.sem, bias_set.at(i, 1))

                def scores_out(n):
                    c, j, h = steps[n]
                    a = col0(c, j)
                    dve.wait_ge(scores.sem, scores.at(i, n + 1))
                    dve.wait_ge(A_ready.sem, A_ready.at(i, n - 3))
                    if j * P >= c * W:
                        ins = nc.vector.scalar_tensor_tensor(out=z[:, n % 4, a:W], in0=Z[n % 2][:, a:W],
                                                             scalar=bias[:, h:h + 1], in1=k.before[:, 0:W - a],
                                                             op0=ALU.add, op1=ALU.min)
                    else:
                        ins = nc.vector.tensor_scalar(z[:, n % 4, a:W], Z[n % 2][:, a:W], bias[:, h:h + 1],
                                                      None, ALU.add)
                    ins.then_inc(z_ready.sem, 1)

                def softplus(n):
                    c, j, h = steps[n]
                    a = col0(c, j)
                    dve.wait_ge(ln_done.sem, ln_done.at(i, n + 1))
                    dve.wait_ge(summed.sem, summed.at(i, n - 2))
                    dve.wait_ge(later_ready.sem, later_ready.at(i, later_count(n - 3) if n >= 3 else n - 2))
                    nc.vector.scalar_tensor_tensor(out=L[:, n % 3, a:W], in0=z[:, n % 4, a:W], scalar=0.0,
                                                   in1=soft[:, n % 2, a:W], op0=ALU.max,
                                                   op1=ALU.add).then_inc(L_ready.sem, 1)

                def exponent(n):
                    c, j, h = steps[n]
                    a = col0(c, j)
                    dve.wait_ge(summed.sem, summed.at(i, n + 1))
                    nc.vector.tensor_tensor(z[:, n % 4, a:W], z[:, n % 4, a:W], SUM[n % 2][:, a:W],
                                            ALU.subtract).then_inc(x_ready.sem, 1)

                def gated(c):
                    dve.wait_ge(weighted.sem, weighted.at(i, NS if c == T // W - 1 else first_of_chunk[c + 1, 0]))
                    m = mix[:, c * W:(c + 1) * W]
                    nc.vector.tensor_tensor(m, Y[:, :], m, ALU.mult).then_inc(y_taken.sem, 1)

                for n in range(NS + 3):
                    if n < NS:
                        scores_out(n)
                    if 1 <= n < NS + 1:
                        softplus(n - 1)
                    if 2 <= n < NS + 2:
                        exponent(n - 2)
                    if n == first_of_chunk[1, 0] + 3:
                        gated(0)
                    if 3 <= n < 5:
                        paged.reduce_keys(dve, i, 11 + n)
                    if n == 5:
                        paged.add_bias(dve, i)
                    if n == 7:
                        paged.softplus(dve, i)
                    if n == 9:
                        paged.exponents(dve, i)
                gated(1)
                paged.take_partial(dve, i)
            paged.result_vector(dve)

        @block.gpsimd
        def _(pool):
            later_ready.credit(pool)
            mix_free.credit(pool)
            paged.setup_pool(pool)
            with pool.Fori(0, GT) as i:
                for r in range(NP):
                    paged.multiply_keys(pool, i, r)
                done = 0
                for n, (c, j, h) in enumerate(steps):
                    a = col0(c, j)
                    pool.wait_ge(L_ready.sem, L_ready.at(i, n + 1))
                    pool.wait_ge(summed.sem, summed.at(i, n + 1))
                    if n == first_of_chunk[c, h]:
                        nc.gpsimd.tensor_tensor(later[:, h, :], k.zeros[:], k.zeros[:],
                                                ALU.add).then_inc(later_ready.sem, 1)
                        done += 1
                    pool.wait_ge(later_ready.sem, later_ready.at(i, done))
                    nc.gpsimd.tensor_tensor(later[:, h, a:W], later[:, h, a:W], L[:, n % 3, a:W],
                                            ALU.add).then_inc(later_ready.sem, 1)
                    done += 1
                pool.wait_ge(y_taken.sem, y_taken.at(i, 2))
                store_mix(nc, pool, k, i + 2 * GT, mix, mix_out, i, mix_free)

        @block.tensor
        def _(pe):
            for s in (proj.projected, tok_turned, scores, summed, weighted):
                s.credit(pe)
            paged.setup_tensor(pe)
            with pe.Fori(0, GT) as i:
                def turn(src, bank, wait):
                    for q in range(2):
                        if q == 0:
                            pe.wait_ge(proj.taken.sem, proj.taken.at(i, wait))
                        for b in range(4):
                            last = nc.tensor.transpose(quad(bank[q])[:, b, :], src[:, (4 * q + b) * P:(4 * q + b + 1) * P],
                                                       k.ident[:])
                        last.then_inc(tok_turned.sem, 1)

                pe.wait_ge(paged.rows_taken.sem, paged.rows_taken.at(i, 0))
                proj.multiply(pe, i, 0)
                proj.multiply(pe, i, 1)
                pe.wait_ge(x_ready.sem, x_ready.at(i, 0))
                turn(vT, SUM, 3)
                proj.multiply(pe, i, 2)
                turn(kT, Z, 6)
                pe.wait_ge(y_taken.sem, y_taken.at(i, 0))
                nc.tensor.transpose(Y[0:NB, 0:P], kT[:, T:NT], k.ident[:])
                nc.tensor.transpose(Y[0:NB, P:2 * P], vT[:, T:NT], k.ident[:]).then_inc(tok_turned.sem, 1)
                proj.multiply(pe, i, 3)
                pe.wait_ge(proj.taken.sem, proj.taken.at(i, 9))
                pe.wait_ge(tok_taken.sem, tok_taken.at(i, 5))

                def score(n):
                    c, j, h = steps[n]
                    a = col0(c, j)
                    pe.wait_ge(z_ready.sem, z_ready.at(i, n - 1))
                    hs = slice(SBD * h, SBD * (h + 1))
                    nc.tensor.matmul(Z[n % 2][:, a:W], kT[hs, j * P:(j + 1) * P], qT[hs, c * W + a:(c + 1) * W],
                                     start=True, stop=True).then_inc(scores.sem, 1)

                def suffix(n):
                    c, j, h = steps[n]
                    a = col0(c, j)
                    first = n == first_of_chunk[c, h]
                    pe.wait_ge(x_ready.sem, x_ready.at(i, n - 1))
                    pe.wait_ge(L_ready.sem, L_ready.at(i, n + 1))
                    last = nc.tensor.matmul(SUM[n % 2][:, a:W], k.from_here[:], L[:, n % 3, a:W],
                                            start=True, stop=first)
                    if not first:
                        pe.wait_ge(later_ready.sem, later_ready.at(i, later_count(n - 2)))
                        last = nc.tensor.matmul(SUM[n % 2][:, a:W], k.ones[:], later[:, h, a:W],
                                                start=False, stop=True)
                    last.then_inc(summed.sem, 1)

                def weigh(n):
                    c, j, h = steps[n]
                    a = col0(c, j)
                    if n == first_of_chunk[c, 0] and c > 0:
                        pe.wait_ge(y_taken.sem, y_taken.at(i, c))
                    pe.wait_ge(A_ready.sem, A_ready.at(i, n + 1))
                    hs = slice(SBD * h, SBD * (h + 1))
                    nc.tensor.matmul(Y[hs, a:W], v_tok[:, j, hs], A[:, n % 3, a:W],
                                     start=(n == first_of_chunk[c, h]), stop=(j == 0),
                                     skip_group_check=True).then_inc(weighted.sem, 1)

                for n in range(NS + 4):
                    if n < NS:
                        score(n)
                    if 2 <= n < NS + 2:
                        suffix(n - 2)
                    if n >= 4:
                        weigh(n - 4)
                    if n == 9:
                        paged.sum_pages(pe, i)
                    if 0 <= n - FIRST_WEIGH < NP:
                        paged.weigh(pe, i, n - FIRST_WEIGH)
            paged.result_tensor(pe)


def constants(nc, ctx, k):
    sb = lambda name, shape, dt=F32: ctx.enter_context(nc.sbuf_tensor(name, shape, dt))
    k.ident = sb("ident", [P, P])
    k.from_here = sb("from_here", [P, P])
    k.ones = sb("ones", [P, P])
    k.before = sb("before", [P, 512])
    k.up_to = sb("up_to", [P, P])
    k.zeros = sb("zeros", [P, 512])
    k.fold = sb("fold", [P, NB])
    k.eps = sb("eps", [P, 1])
    filled = nc.alloc_semaphore("constants_filled")
    with nc.Block() as block:

        @block.gpsimd
        def _(pool):
            for tile, value in ((k.ident, 0.0), (k.from_here, 1.0), (k.ones, 1.0), (k.before, BIG),
                                (k.up_to, 0.0), (k.zeros, 0.0), (k.eps, EPS), (k.fold, 0.0)):
                nc.gpsimd.memset(tile[:], value).then_inc(filled, 1)
            pool.wait_ge(filled, 8)
            nc.gpsimd.affine_select(out=k.ident[:], in_=k.ident[:], compare_op=ALU.not_equal, fill=1.0,
                                    base=0, pattern=[[-1, P]], channel_multiplier=1).then_inc(filled, 1)
            nc.gpsimd.affine_select(out=k.from_here[:], in_=k.from_here[:], compare_op=ALU.is_ge, fill=0.0,
                                    base=0, pattern=[[-1, P]], channel_multiplier=1).then_inc(filled, 1)
            nc.gpsimd.affine_select(out=k.before[:], in_=k.before[:], compare_op=ALU.is_gt, fill=FAR,
                                    base=0, pattern=[[1, 512]], channel_multiplier=-1).then_inc(filled, 1)
            nc.gpsimd.affine_select(out=k.up_to[:], in_=k.up_to[:], compare_op=ALU.is_ge, fill=FAR,
                                    base=0, pattern=[[1, P]], channel_multiplier=-1).then_inc(filled, 1)
            for g in range(4):
                nc.gpsimd.affine_select(out=k.fold[:], in_=k.fold[:], compare_op=ALU.not_equal, fill=1.0, base=-32 * g,
                                        pattern=[[-1, NB]], channel_multiplier=1).then_inc(filled, 1)
                pool.wait_ge(filled, 13 + g)


def memory_keys(nc, ctx, k):
    sb = lambda name, shape, dt=F32: ctx.enter_context(nc.sbuf_tensor("m_" + name, shape, dt))
    S = lambda name, per, unit=1: Signal(ctx, nc, "m_" + name, per, unit)
    mh, ml = sb("hi", [P, KT, NMEM], F32R), sb("lo", [P, KT, NMEM], F32R)
    quad = lambda bank: bank[:, :].rearrange("p (b t) -> p b t", b=4)
    rows = k.mem_prompt.rearrange("o (r p) d -> (o r) p d", p=P)
    with ExitStack() as inner:
        normalise_and_transpose(nc, inner, "mn", [(rows[r], P, r * P) for r in range(NMEM // P)], k.mem_norm,
                                mh, ml, k.ident, k.eps, [quad(b) for b in k.bank])
    proj = Projection(ctx, nc, "m", 2, 2, mh, ml, k.bank[0:1], width=NMEM)
    kT, vT, tok = sb("kT", [P, NMEM]), sb("vT", [P, NMEM]), sb("tok", [P, 4, P])
    turned, tok_taken, kept = S("turned", 1), S("tok_taken", 1), S("kept", 2)
    out_done, written = S("out_done", 2, 16), S("written", 1)
    sending = nc.alloc_semaphore("m_sending")
    with nc.Block() as block:

        @block.sync
        def _(sp):
            written.credit(sp)
            with sp.Fori(0, MLH) as i:
                first = [sp.snap(i * P + base) for base in (0, GW)]
                for j in range(2):
                    proj.load(sp, i, j, k.w_mem[:, :, bass.ds(first[j], P)])
                sp.wait_ge(tok_taken.sem, tok_taken.at(i, 1))
                sp.sem_inc(sending, 1)
                sp.dma_start(k.mem_k[:, :, bass.ds(i * P, P)], tok[:, 0:2, :]).then_inc(out_done.sem, 16)
                sp.dma_start(k.mem_v[:, :, bass.ds(i * P, P)], tok[:, 2:4, :]).then_inc(out_done.sem, 16)
                sp.wait_ge(out_done.sem, out_done.at(i, 2))
                sp.sem_inc(written.sem, 1)

        @block.scalar
        def _(act):
            for s in (proj.hi_ready, proj.taken):
                s.credit(act)
            with act.Fori(0, MLH) as i:
                proj.split_hi(act, i, 0)
                proj.split_hi(act, i, 1)
                act.wait_ge(kept.sem, kept.at(i, 0))
                proj.take(act, i, 0, lambda c: kT[:], ACT.Copy)
                proj.take(act, i, 1, lambda c: vT[:], ACT.Copy)

        @block.vector
        def _(dve):
            for s in (proj.lo_ready, tok_taken, kept):
                s.credit(dve)
            with dve.Fori(0, MLH) as i:
                proj.split_lo(dve, i, 0)
                proj.split_lo(dve, i, 1)
                dve.wait_ge(proj.taken.sem, proj.taken.at(i, 1))
                nc.vector.tensor_copy(k.mem_kT[:, bass.ds(i, 1), :].rearrange("p a t -> p (a t)"), kT[:]).then_inc(kept.sem, 1)
                dve.wait_ge(turned.sem, turned.at(i, 1))
                dve.wait_ge(written.sem, written.at(i, 0))
                nc.vector.tensor_copy(tok[:], quad(k.bank[3])).then_inc(tok_taken.sem, 1)
                nc.vector.tensor_copy(k.mem_v_tok[:, bass.ds(i, 1)].rearrange("p a b d -> p (a b) d"),
                                      quad(k.bank[3])[:, 2:4, :]).then_inc(kept.sem, 1)

        @block.tensor
        def _(pe):
            for s in (proj.projected, turned):
                s.credit(pe)
            with pe.Fori(0, MLH) as i:
                proj.multiply(pe, i, 0)
                proj.multiply(pe, i, 1)
                pe.wait_ge(proj.taken.sem, proj.taken.at(i, 2))
                pe.wait_ge(kept.sem, kept.at(i, 0))
                for n, src in enumerate((kT, vT)):
                    for b in range(2):
                        last = nc.tensor.transpose(quad(k.bank[3])[:, 2 * n + b, :], src[:, b * P:(b + 1) * P], k.ident[:])
                last.then_inc(turned.sem, 1)


def memory_and_pooling(nc, ctx, k):
    sb = lambda name, shape, dt=F32: ctx.enter_context(nc.sbuf_tensor("d_" + name, shape, dt))
    S = lambda name, per, unit=1: Signal(ctx, nc, "d_" + name, per, unit)
    sem = lambda name: nc.alloc_semaphore("d_" + name)
    proj = Projection(ctx, nc, "d", 4, 2, k.xh, k.xl, k.bank[0:3])
    UNITS, UB = TB // 2, 2
    UT = UB * P
    PAD = 2 ** MLH
    MB = NMEM // P
    qT = sb("qT", [P, NT])
    kT, v_tok = sb("kT", [P, NMEM]), sb("v_tok", [P, MB, P])
    prob, probT = sb("prob", [P, 2, UB, NMEM]), sb("probT", [P, 2, MB, UT])
    top, total, inv = sb("top", [P, 2, UB]), sb("total", [P, 2, UB]), sb("inv", [P, 2, UB])
    q_diag = probT[:].rearrange("p s m t -> p (s m t)").rearrange("p (b d) -> p b d", b=NB)
    cache = sb("cache", [P, NB, MB, P])
    s_col, new_prob = sb("s_col", [P, MB, NB]), sb("new_prob", [NB, NMEM])
    new_top, new_total, new_inv = sb("new_top", [NB, 1]), sb("new_total", [NB, 1]), sb("new_inv", [NB, 1])
    new_probT = sb("new_probT", [P, MB, NB])
    u = sb("u", [P, PAD + NT])
    sums = [sb("sums0", [P, PAD + T]), sb("sums1", [P, PAD + T])]
    pooled = sums[0]
    mix_d, mix_a = sb("mix_d", [P, NT]), sb("mix_a", [P, NT])
    pooled_new = sb("pooled_new", [P, NB])
    buf_rows = sb("buf_rows", [NB * POOL_BUF, P])
    new_sums = [sb(f"new_sums{n}", [P, NB, PAD]) for n in range(2)]
    edge = sb("edge", [P, PAD])
    inv_count, adds = sb("inv_count", [P, MLH, PAD]), sb("adds", [P, MLH, MLH])
    inv_count_g, adds_g = sb("inv_count_g", [P, PAD]), sb("adds_g", [P, MLH])
    scale_all, scale = sb("scale_all", [P, MLH]), sb("scale", [P, 1])
    pool_w = sb("pool_w", [P, P])
    out_rows = sb("out_rows", [POOL_BUF + NB, P])
    NO = POOL_BUF + NB

    quad = lambda bank: bank[:, :].rearrange("p (b t) -> p b t", b=4)
    pair = lambda bank: bank[:, :].rearrange("p (b t) -> p b t", b=2)
    B3, B4, B5, B6, B7 = k.bank[3:8]
    SC, TP = (B3, B4), (B5, B6)
    tables_set, scale_in, sending, bufs_moved = sem("tables_set"), sem("scale_in"), sem("sending"), sem("bufs_moved")
    small_in, keys_in, values_in = S("small_in", 2, 16), S("keys_in", 1, 16), S("values_in", 1, 16)
    small_set = S("small_set", 5)
    scored, top_ready, neg_ready, exp_done = S("scored", UNITS), S("top_ready", UNITS), S("neg_ready", UNITS), S("exp_done", UNITS)
    inv_ready, prob_ready, turned, turned_taken = S("inv_ready", UNITS), S("prob_ready", UNITS), S("turned", UNITS), S("turned_taken", UNITS)
    weighted, y_taken = S("weighted", UNITS), S("y_taken", 2)
    diag_ready, q_spread, product_ready, s_ready, s_turned = S("diag_ready", 1), S("q_spread", 1), S("product_ready", 2), S("s_ready", 1), S("s_turned", 1)
    new_step, new_exp, new_back, new_taken = S("new_step", 4), S("new_exp", 1), S("new_back", 1), S("new_taken", 1)
    new_weighted, new_gated = S("new_weighted", 1), S("new_gated", 1)
    buf_turned, buf_taken, u_turned, u_rows = S("buf_turned", 1), S("buf_taken", 2), S("u_turned", 1), S("u_rows", 1)
    doubled, pooled_ready = S("doubled", 2 * MLH), S("pooled_ready", 4)
    pool_done, pool_mixed = S("pool_done", 3), S("pool_mixed", 3)
    out_done, written = S("out_done", 2, 16), S("written", 1)
    d_out, a_out, d_free, a_free = S("d_out", 1, 16), S("a_out", 1, 16), S("d_free", 2), S("a_free", 2)

    with nc.Block() as block:

        @block.sync
        def _(sp):
            sp.dma_start(scale_all[:], k.pool_scale, allow_slow_non_contiguous=True).then_inc(scale_in, 16)
            sp.dma_start(k.pool_sample[:, 0:POOL_BUF - 1, :], k.state_pool[:, 1:POOL_BUF, :]).then_inc(bufs_moved, 16)
            written.credit(sp)
            with sp.Fori(0, MLH) as i:
                first = [sp.snap(i * P + base) for base in (D_Q, D_G, A_U, A_G)]
                proj.load(sp, i, 0, k.w_in[:, :, bass.ds(first[0], P)])
                sp.wait_ge(new_weighted.sem, new_weighted.at(i, 0))
                sp.sem_inc(sending, 1)
                sp.dma_start(cache[:].rearrange("p b m d -> p (b m) d"),
                             k.cache_mem_k[:, :, bass.ds(i * P, P)]).then_inc(keys_in.sem, 16)
                proj.load(sp, i, 1, k.w_in[:, :, bass.ds(first[1], P)])
                sp.wait_ge(pool_done.sem, pool_done.at(i, 0))
                sp.sem_inc(sending, 1)
                sp.dma_start(pool_w[:], k.pool_w[:, bass.ds(i, 1), :].rearrange("p a d -> p (a d)")).then_inc(small_in.sem, 16)
                sp.dma_start(buf_rows[:], k.state_pool.rearrange("b r c -> (b r) c")[:, bass.ds(i * P, P)]).then_inc(small_in.sem, 16)
                proj.load(sp, i, 2, k.w_in[:, :, bass.ds(first[2], P)])
                proj.load(sp, i, 3, k.w_in[:, :, bass.ds(first[3], P)])
                sp.wait_ge(s_ready.sem, s_ready.at(i, 1))
                sp.sem_inc(sending, 1)
                sp.dma_start(cache[:].rearrange("p b m d -> p (b m) d"),
                             k.cache_mem_v[:, :, bass.ds(i * P, P)]).then_inc(values_in.sem, 16)
                sp.wait_ge(u_rows.sem, u_rows.at(i, 1))
                sp.sem_inc(sending, 1)
                sp.dma_start(k.pool_prompt[:, bass.ds(i * P, P)], out_rows[0:POOL_BUF, :]).then_inc(out_done.sem, 16)
                sp.dma_start(k.pool_sample[:, POOL_BUF - 1, bass.ds(i * P, P)], out_rows[POOL_BUF:NO, :]).then_inc(out_done.sem, 16)
                sp.wait_ge(out_done.sem, out_done.at(i, 2))
                sp.sem_inc(written.sem, 1)
            sp.wait_ge(bufs_moved, 16)

        @block.gpsimd
        def _(pool):
            n = 0
            for value, dst in [(1.0 / (t + 1), inv_count[:, :, t:t + 1]) for t in range(PAD)] + \
                    [(0.0, adds[:]), (0.0, u[:, 0:PAD]), (0.0, sums[0][:, 0:PAD]), (0.0, sums[1][:, 0:PAD])]:
                nc.gpsimd.memset(dst, value).then_inc(tables_set, 1)
                n += 1
            pool.wait_ge(tables_set, n)
            for g in range(MLH):
                if 2 ** (g + 1) < PAD:
                    nc.gpsimd.memset(inv_count[:, g, 2 ** (g + 1):PAD], 0.5 ** (g + 1)).then_inc(tables_set, 1)
                nc.gpsimd.memset(adds[:, g, 0:g + 1], 1.0).then_inc(tables_set, 1)
            d_free.credit(pool)
            a_free.credit(pool)
            with pool.Fori(0, MLH) as i:
                pool.wait_ge(y_taken.sem, y_taken.at(i, 2))
                store_mix(nc, pool, k, i + 3 * GT, mix_d, d_out, i, d_free)
                pool.wait_ge(pool_mixed.sem, pool_mixed.at(i, 2))
                store_mix(nc, pool, k, i, mix_a, a_out, i, a_free)
        TABLES = PAD + 4 + 2 * MLH - 1

        @block.scalar
        def _(act):
            for s in (proj.hi_ready, proj.taken, exp_done, new_exp):
                s.credit(act)
            act.wait_ge(tables_set, TABLES)
            with act.Fori(0, MLH) as i:
                def exponent(n):
                    s = n % 2
                    act.wait_ge(neg_ready.sem, neg_ready.at(i, n + 1))
                    act.wait_ge(turned.sem, turned.at(i, n - 1))
                    act.wait_ge(inv_ready.sem, inv_ready.at(i, n - 1))
                    for b in range(UB):
                        last = nc.scalar.activation(prob[:, s, b, :], pair(SC[s])[:, b, :], ACT.Exp,
                                                    bias=top[:, s, b:b + 1], accum_out=total[:, s, b:b + 1])
                    last.then_inc(exp_done.sem, 1)

                proj.split_hi(act, i, 0)
                proj.split_hi(act, i, 1)
                act.wait_ge(weighted.sem, weighted.at(i, 0))
                act.wait_ge(new_weighted.sem, new_weighted.at(i, 0))
                proj.take(act, i, 0, lambda c: qT[:, c * CH:(c + 1) * CH], ACT.Copy, scale=DK ** -0.5)
                proj.split_hi(act, i, 2)
                load_tables(nc, act, LN_EXP)
                exponent(0)
                exponent(1)
                act.wait_ge(d_free.sem, d_free.at(i, 0))
                act.wait_ge(new_gated.sem, new_gated.at(i, 0))
                proj.take(act, i, 1, lambda c: mix_d[:, c * CH:(c + 1) * CH], ACT.Silu)
                proj.split_hi(act, i, 3)
                load_tables(nc, act, LN_EXP)
                act.wait_ge(new_step.sem, new_step.at(i, 2))
                nc.scalar.activation(new_prob[:], B7[0:NB, 0:NMEM], ACT.Exp, bias=new_top[:],
                                     accum_out=new_total[:]).then_inc(new_exp.sem, 1)
                exponent(2)
                exponent(3)
                act.wait_ge(pool_mixed.sem, pool_mixed.at(i, 0))
                act.wait_ge(pooled_ready.sem, pooled_ready.at(i, 0))
                proj.take(act, i, 2, lambda c: u[:, PAD + c * CH:PAD + (c + 1) * CH], ACT.Copy)
                act.wait_ge(a_free.sem, a_free.at(i, 0))
                proj.take(act, i, 3, lambda c: mix_a[:, c * CH:(c + 1) * CH], ACT.Silu)

        @block.vector
        def _(dve):
            for s in (proj.lo_ready, small_set, top_ready, neg_ready, inv_ready, prob_ready, turned_taken, y_taken,
                      diag_ready, product_ready, s_ready, new_step, new_taken, new_gated, buf_taken, u_rows, doubled,
                      pooled_ready, pool_mixed):
                s.credit(dve)
            dve.wait_ge(scale_in, 16)
            dve.wait_ge(tables_set, TABLES)
            with dve.Fori(0, MLH) as i:
                def maximum(n):
                    s = n % 2
                    dve.wait_ge(scored.sem, scored.at(i, n + 1))
                    nc.vector.tensor_reduce(inv[:, s, :], pair(SC[s]), AXX, ALU.max).then_inc(top_ready.sem, 1)
                    dve.wait_ge(top_ready.sem, top_ready.at(i, n + 1))
                    nc.vector.tensor_scalar(top[:, s, :], inv[:, s, :], -1.0, None, ALU.mult).then_inc(neg_ready.sem, 1)

                def normalised(n):
                    s = n % 2
                    dve.wait_ge(exp_done.sem, exp_done.at(i, n + 1))
                    dve.wait_ge(neg_ready.sem, neg_ready.at(i, n + 1))
                    nc.vector.reciprocal(inv[:, s, :], total[:, s, :]).then_inc(inv_ready.sem, 1)
                    dve.wait_ge(inv_ready.sem, inv_ready.at(i, n + 1))
                    for b in range(UB):
                        last = nc.vector.tensor_scalar(prob[:, s, b, :], prob[:, s, b, :], inv[:, s, b:b + 1], None, ALU.mult)
                    last.then_inc(prob_ready.sem, 1)

                def take_turned(n):
                    dve.wait_ge(turned.sem, turned.at(i, n + 1))
                    dve.wait_ge(weighted.sem, weighted.at(i, n - 1))
                    nc.vector.tensor_copy(probT[:, n % 2], pair(TP[n % 2])).then_inc(turned_taken.sem, 1)

                def gated(half):
                    dve.wait_ge(weighted.sem, weighted.at(i, 2 * half + 2))
                    m = mix_d[:, 2 * half * UT:2 * (half + 1) * UT]
                    nc.vector.tensor_tensor(m, B7[:, :], m, ALU.mult).then_inc(y_taken.sem, 1)

                proj.split_lo(dve, i, 0)
                proj.split_lo(dve, i, 1)
                dve.wait_ge(weighted.sem, weighted.at(i, 0))
                dve.wait_ge(pool_mixed.sem, pool_mixed.at(i, 0))
                nc.vector.tensor_copy(kT[:], k.mem_kT[:, bass.ds(i, 1), :].rearrange("p a t -> p (a t)")).then_inc(small_set.sem, 1)
                nc.vector.tensor_copy(v_tok[:], k.mem_v_tok[:, bass.ds(i, 1)].rearrange("p a b d -> p (a b) d")).then_inc(small_set.sem, 1)
                nc.vector.tensor_copy(inv_count_g[:], inv_count[:, bass.ds(i, 1), :].rearrange("p a t -> p (a t)")).then_inc(small_set.sem, 1)
                nc.vector.tensor_copy(adds_g[:], adds[:, bass.ds(i, 1), :].rearrange("p a t -> p (a t)")).then_inc(small_set.sem, 1)
                nc.vector.tensor_copy(scale[:], scale_all[:, bass.ds(i, 1)]).then_inc(small_set.sem, 1)
                dve.wait_ge(proj.taken.sem, proj.taken.at(i, 3))
                for b in range(NB):
                    last = nc.vector.tensor_scalar(q_diag[:, b, :], k.ident[:], qT[:, T + b:T + b + 1], None, ALU.mult)
                last.then_inc(diag_ready.sem, 1)
                maximum(0)
                maximum(1)
                proj.split_lo(dve, i, 2)
                dve.wait_ge(keys_in.sem, keys_in.at(i, 1))
                dve.wait_ge(q_spread.sem, q_spread.at(i, 1))
                for g in range(2):
                    q = quad((B5, B6)[g]).rearrange("p b (o d) -> p b o d", o=1).to_broadcast([P, 4, MB, P])
                    nc.vector.tensor_tensor(cache[:, 4 * g:4 * g + 4], cache[:, 4 * g:4 * g + 4], q,
                                            ALU.mult).then_inc(product_ready.sem, 1)
                dve.wait_ge(product_ready.sem, product_ready.at(i, 2))
                nc.vector.tensor_reduce(s_col[:].rearrange("p m b -> p b m"), cache[:], AXX, ALU.add).then_inc(s_ready.sem, 1)
                normalised(0)
                normalised(1)
                proj.split_lo(dve, i, 3)
                dve.wait_ge(s_turned.sem, s_turned.at(i, 1))
                nc.vector.tensor_reduce(new_inv[:], B7[0:NB, 0:NMEM], AXX, ALU.max).then_inc(new_step.sem, 1)
                dve.wait_ge(new_step.sem, new_step.at(i, 1))
                nc.vector.tensor_scalar(new_top[:], new_inv[:], -1.0, None, ALU.mult).then_inc(new_step.sem, 1)
                take_turned(0)
                take_turned(1)
                maximum(2)
                maximum(3)
                dve.wait_ge(new_exp.sem, new_exp.at(i, 1))
                dve.wait_ge(new_step.sem, new_step.at(i, 2))
                nc.vector.reciprocal(new_inv[:], new_total[:]).then_inc(new_step.sem, 1)
                dve.wait_ge(new_step.sem, new_step.at(i, 3))
                nc.vector.tensor_scalar(new_prob[:], new_prob[:], new_inv[:], None, ALU.mult).then_inc(new_step.sem, 1)
                normalised(2)
                normalised(3)
                dve.wait_ge(buf_turned.sem, buf_turned.at(i, 1))
                dve.wait_ge(new_back.sem, new_back.at(i, 1))
                dve.wait_ge(u_turned.sem, u_turned.at(i, 1))
                nc.vector.tensor_copy(new_sums[0][:, :, 0:POOL_BUF],
                                      B3[:, 0:NB * POOL_BUF].rearrange("p (b r) -> p b r", b=NB)).then_inc(buf_taken.sem, 1)
                nc.vector.tensor_copy(new_sums[0][:, :, POOL_BUF:PAD],
                                      u[:, PAD + T:PAD + NT].rearrange("p (b o) -> p b o", o=1)).then_inc(buf_taken.sem, 1)
                nc.vector.tensor_copy(new_probT[:].rearrange("p m b -> p (m b)"), B3[:, 256:256 + MB * NB]).then_inc(new_taken.sem, 1)
                dve.wait_ge(written.sem, written.at(i, 0))
                nc.vector.tensor_copy(out_rows[:], B3[0:NO, P:2 * P]).then_inc(u_rows.sem, 1)
                take_turned(2)
                take_turned(3)
                gated(0)
                dve.wait_ge(small_set.sem, small_set.at(i, 5))
                dve.wait_ge(buf_taken.sem, buf_taken.at(i, 2))
                for d in range(MLH):
                    dve.wait_ge(doubled.sem, doubled.at(i, 2 * d))
                    sh = 2 ** d
                    src = u if d == 0 else sums[(d + 1) % 2]
                    nc.vector.scalar_tensor_tensor(out=sums[d % 2][:, PAD:PAD + T], in0=src[:, PAD - sh:PAD + T - sh],
                                                   scalar=adds_g[:, d:d + 1], in1=src[:, PAD:PAD + T],
                                                   op0=ALU.mult, op1=ALU.add).then_inc(doubled.sem, 1)
                    nsrc = new_sums[d % 2]
                    nc.vector.scalar_tensor_tensor(out=new_sums[(d + 1) % 2][:, :, 2 * sh - 1:PAD], in0=nsrc[:, :, sh - 1:PAD - sh],
                                                   scalar=adds_g[:, d:d + 1], in1=nsrc[:, :, 2 * sh - 1:PAD],
                                                   op0=ALU.mult, op1=ALU.add).then_inc(doubled.sem, 1)
                dve.wait_ge(doubled.sem, doubled.at(i, 2 * MLH))
                whole = inv_count_g[:, PAD - 1:PAD]
                nc.vector.tensor_tensor(edge[:], sums[1][:, PAD:2 * PAD], inv_count_g[:], ALU.mult).then_inc(pooled_ready.sem, 1)
                nc.vector.scalar_tensor_tensor(out=pooled[:, 2 * PAD:PAD + T], in0=sums[1][:, 2 * PAD:PAD + T], scalar=whole,
                                               in1=u[:, 2 * PAD:PAD + T], op0=ALU.mult, op1=ALU.subtract)\
                    .then_inc(pooled_ready.sem, 1)
                nc.vector.scalar_tensor_tensor(out=pooled_new[:], in0=new_sums[0][:, :, PAD - 1], scalar=whole,
                                               in1=u[:, PAD + T:PAD + NT], op0=ALU.mult, op1=ALU.subtract)\
                    .then_inc(pooled_ready.sem, 1)
                dve.wait_ge(pooled_ready.sem, pooled_ready.at(i, 1))
                nc.vector.tensor_tensor(pooled[:, PAD:2 * PAD], edge[:], u[:, PAD:2 * PAD], ALU.subtract).then_inc(pooled_ready.sem, 1)
                gated(1)
                dve.wait_ge(new_weighted.sem, new_weighted.at(i, 1))
                new_mix = lambda group: k.new_mix[:, bass.ds(i + group * GT, 1), :].rearrange("p a b -> p (a b)")
                nc.vector.tensor_tensor(new_mix(3), B4[:, 0:NB], mix_d[:, T:NT], ALU.mult).then_inc(new_gated.sem, 1)
                dve.wait_ge(proj.taken.sem, proj.taken.at(i, 12))
                for c, (bank, a, b) in enumerate(((B5, 0, 512), (B6, 512, T), (B3, T, NT))):
                    dve.wait_ge(pool_done.sem, pool_done.at(i, c + 1))
                    m = mix_a[:, a:b]
                    nc.vector.scalar_tensor_tensor(out=m if c < 2 else new_mix(0), in0=bank[:, 0:b - a], scalar=scale[:], in1=m,
                                                   op0=ALU.mult, op1=ALU.mult).then_inc(pool_mixed.sem, 1)

        @block.tensor
        def _(pe):
            for s in (proj.projected, scored, turned, weighted, q_spread, s_turned, new_back, new_weighted,
                      buf_turned, u_turned, pool_done):
                s.credit(pe)
            with pe.Fori(0, MLH) as i:
                def score(n):
                    pe.wait_ge(exp_done.sem, exp_done.at(i, n - 1))
                    for b in range(UB):
                        t0 = (UB * n + b) * P
                        last = nc.tensor.matmul(pair(SC[n % 2])[:, b, :], qT[:, t0:t0 + P], kT[:], start=True, stop=True)
                    last.then_inc(scored.sem, 1)

                def turn(n):
                    pe.wait_ge(prob_ready.sem, prob_ready.at(i, n + 1))
                    pe.wait_ge(turned_taken.sem, turned_taken.at(i, n - 1))
                    for m in range(MB):
                        for b in range(UB):
                            last = nc.tensor.transpose(pair(TP[n % 2])[:, m, b * P:(b + 1) * P],
                                                       prob[:, n % 2, b, m * P:(m + 1) * P], k.ident[:])
                    last.then_inc(turned.sem, 1)

                def weigh(n):
                    pe.wait_ge(turned_taken.sem, turned_taken.at(i, n + 1))
                    if n % 2 == 0:
                        pe.wait_ge(y_taken.sem, y_taken.at(i, n // 2))
                    for m in range(MB):
                        last = nc.tensor.matmul(pair(B7)[:, n % 2, :], v_tok[:, m, :], probT[:, n % 2, m, :],
                                                start=(m == 0), stop=(m == MB - 1))
                    last.then_inc(weighted.sem, 1)

                proj.multiply(pe, i, 0)
                pe.wait_ge(small_set.sem, small_set.at(i, 2))
                pe.wait_ge(proj.taken.sem, proj.taken.at(i, 3))
                pe.wait_ge(pool_mixed.sem, pool_mixed.at(i, 0))
                pe.wait_ge(new_gated.sem, new_gated.at(i, 0))
                score(0)
                score(1)
                pe.wait_ge(diag_ready.sem, diag_ready.at(i, 1))
                for g in range(2):
                    last = nc.tensor.matmul((B5, B6)[g][:, :], k.ones[:], q_diag[:, 4 * g:4 * g + 4, :]
                                            .rearrange("p b d -> p (b d)"), start=True, stop=True)
                last.then_inc(q_spread.sem, 1)
                proj.multiply(pe, i, 1)
                pe.wait_ge(s_ready.sem, s_ready.at(i, 1))
                pe.wait_ge(y_taken.sem, y_taken.at(i, 0))
                for m in range(MB):
                    last = nc.tensor.transpose(B7[0:NB, m * P:(m + 1) * P], s_col[:, m, :], k.ident[:])
                last.then_inc(s_turned.sem, 1)
                turn(0)
                turn(1)
                score(2)
                score(3)
                proj.multiply(pe, i, 2)
                turn(2)
                turn(3)
                pe.wait_ge(exp_done.sem, exp_done.at(i, 3))
                pe.wait_ge(small_in.sem, small_in.at(i, 2))
                nc.tensor.transpose(B3[:, 0:NB * POOL_BUF], buf_rows[:], k.ident[0:NB * POOL_BUF, 0:NB * POOL_BUF])\
                    .then_inc(buf_turned.sem, 1)
                pe.wait_ge(new_step.sem, new_step.at(i, 4))
                pe.wait_ge(proj.taken.sem, proj.taken.at(i, 9))
                nc.tensor.transpose(B3[0:NO, P:2 * P], u[:, PAD + T - POOL_BUF:PAD + NT], k.ident[:]).then_inc(u_turned.sem, 1)
                for m in range(MB):
                    last = nc.tensor.transpose(B3[:, 256 + m * NB:256 + (m + 1) * NB], new_prob[:, m * P:(m + 1) * P],
                                               k.ident[0:NB, 0:NB])
                last.then_inc(new_back.sem, 1)
                weigh(0)
                weigh(1)
                proj.multiply(pe, i, 3)
                weigh(2)
                weigh(3)
                pe.wait_ge(new_taken.sem, new_taken.at(i, 1))
                pe.wait_ge(values_in.sem, values_in.at(i, 1))
                pe.wait_ge(exp_done.sem, exp_done.at(i, 4))
                for b in range(NB):
                    for m in range(MB):
                        last = nc.tensor.matmul(B4[:, b:b + 1], cache[:, b, m, :], new_probT[:, m, b:b + 1],
                                                start=(m == 0), stop=(m == MB - 1))
                last.then_inc(new_weighted.sem, 1)
                pe.wait_ge(pooled_ready.sem, pooled_ready.at(i, 4))
                pe.wait_ge(u_rows.sem, u_rows.at(i, 1))
                for bank, src in ((B5, pooled[:, PAD:PAD + 512]), (B6, pooled[:, PAD + 512:PAD + T]), (B3, pooled_new[:])):
                    nc.tensor.matmul(bank[:, 0:src.shape[-1]], pool_w[:], src, start=True, stop=True).then_inc(pool_done.sem, 1)


def mlstm_gates(nc, ctx, k):
    sb = lambda name, shape, dt=F32: ctx.enter_context(nc.sbuf_tensor("g_" + name, shape, dt))
    sem = lambda name: nc.alloc_semaphore("g_" + name)
    proj = Projection(ctx, nc, "g", 1, 1, k.xh, k.xl, k.bank[0:3])
    G = 2 * MLH
    R = MLH * TB
    gates, biased, gate_bias = sb("gates", [P, NT]), sb("biased", [G, NT]), sb("gate_bias", [G, 1])
    i_row, f_row = sb("i_row", [R, P]), sb("f_row", [R, P])
    soft, logf, b, a, top = (sb(n, [R, P]) for n in ("soft", "logf", "b", "a", "top"))
    out_rows = sb("out_rows", [R, 3, P])
    ends = sb("ends", [R, 2])
    end_rows = sb("end_rows", [1, 2, R])
    m_row = sb("m_row", [1, MLH, TB + 1])
    m_prev_row = sb("m_prev_row", [1, R])
    m_prev = sb("m_prev", [R, 1])
    new = sb("new", [NB, G])
    m_old, new_soft, new_logf = sb("m_old", [NB, MLH]), sb("new_soft", [NB, MLH]), sb("new_logf", [NB, MLH])
    carried, m_new, new_diff = sb("carried", [NB, MLH]), sb("m_new", [NB, MLH]), sb("new_diff", [NB, 2, MLH])
    new_out = sb("new_out", [NB, 3, MLH])
    n_rows = sb("n_rows", [NB * MLH, P])
    loaded, biased_done, to_dram, from_dram = sem("loaded"), sem("biased"), sem("to_dram"), sem("from_dram")
    dve_new, act_new = sem("dve_new"), sem("act_new")
    dve_row, act_row = sem("dve_row"), sem("act_row")
    turned = sem("turned")
    results_out = sem("results_out")
    tiny = k.bank[3]
    with nc.Block() as block:

        @block.sync
        def _(sp):
            sp.dma_start(gate_bias[:], k.gate_bias, allow_slow_non_contiguous=True).then_inc(loaded, 16)
            sp.dma_start(m_old[:], k.state_m).then_inc(loaded, 16)
            sp.dma_start(n_rows[:], k.state_n).then_inc(loaded, 16)
            proj.load(sp, 0, 0, k.w_in[:, :, B_IF:B_IF + P])
            sp.wait_ge(biased_done, 2)
            sp.dma_start(k.gates_dram, biased[:, 0:T]).then_inc(to_dram, 16)
            sp.dma_start(k.new_gates_dram, biased[:, T:NT]).then_inc(to_dram, 16)
            sp.wait_ge(to_dram, 32)
            sp.dma_start(i_row[:], k.gates_dram[0:MLH, :].rearrange("h (c t) -> (h c) t", t=P)).then_inc(from_dram, 16)
            sp.dma_start(f_row[:], k.gates_dram[MLH:G, :].rearrange("h (c t) -> (h c) t", t=P)).then_inc(from_dram, 16)
            sp.dma_start(new[:], k.new_gates_dram.rearrange("g b -> b g"),
                         allow_slow_non_contiguous=True).then_inc(from_dram, 16)
            sp.wait_ge(dve_new, 4)
            sp.dma_start(k.m_sample, m_new[:]).then_inc(results_out, 16)
            sp.wait_ge(act_new, 5)
            sp.dma_start(k.new_rows_dram, new_out[:].rearrange("b k h -> b (k h)")).then_inc(results_out, 16)
            sp.wait_ge(dve_row, 10)
            sp.dma_start(k.m_prompt, m_row[:, :, TB:TB + 1].rearrange("o h c -> o (h c)"),
                         allow_slow_non_contiguous=True).then_inc(results_out, 16)
            sp.wait_ge(act_row, 5)
            sp.wait_ge(dve_row, 15)
            sp.dma_start(k.rows_dram.rearrange("k h (c t) -> (h c) k t", t=P), out_rows[:]).then_inc(results_out, 16)
            sp.wait_ge(results_out, 64)

        @block.scalar
        def _(act):
            for s in (proj.hi_ready, proj.taken):
                s.credit(act)
            load_tables(nc, act, LN_EXP)
            proj.split_hi(act, 0, 0)
            proj.take(act, 0, 0, lambda c: gates[:, c * CH:(c + 1) * CH], ACT.Copy)
            act.wait_ge(from_dram, 48)
            for dst, src, s in ((soft, f_row[:], act_row), (new_soft, new[:, MLH:G], act_new)):
                nc.scalar.activation(dst[:], src, ACT.Abs).then_inc(s, 1)
                act.wait_ge(s, 1)
                nc.scalar.activation(dst[:], dst[:], ACT.Exp, scale=-1.0).then_inc(s, 1)
                act.wait_ge(s, 2)
                nc.scalar.activation(dst[:], dst[:], ACT.Ln, bias=1.0).then_inc(s, 1)
            act.wait_ge(dve_new, 6)
            nc.scalar.activation(new_out[:, 0:2, :], new_diff[:], ACT.Exp).then_inc(act_new, 1)
            nc.scalar.activation(new_out[:, 2, :], m_new[:], ACT.Exp, scale=-1.0).then_inc(act_new, 1)
            act.wait_ge(dve_row, 13)
            nc.scalar.activation(out_rows[:, 1, :], top[:], ACT.Exp, scale=-1.0, bias=m_prev[:]).then_inc(act_row, 1)
            act.wait_ge(dve_row, 15)
            nc.scalar.activation(out_rows[:, 2, :], b[:], ACT.Exp, scale=-1.0).then_inc(act_row, 1)

        @block.vector
        def _(dve):
            proj.lo_ready.credit(dve)
            proj.split_lo(dve, 0, 0)
            nc.vector.memset(m_row[:], 0.0).then_inc(biased_done, 1)
            dve.wait_ge(biased_done, 1)
            dve.wait_ge(loaded, 48)
            dve.wait_ge(proj.taken.sem, proj.taken.at(0, 3))
            nc.vector.tensor_scalar(biased[:], gates[0:G, :], gate_bias[:], None, ALU.add).then_inc(biased_done, 1)
            dve.wait_ge(act_row, 3)
            nc.vector.scalar_tensor_tensor(out=logf[:], in0=f_row[:], scalar=0.0, in1=soft[:],
                                           op0=ALU.min, op1=ALU.subtract).then_inc(dve_row, 1)
            dve.wait_ge(dve_row, 1)
            nc.vector.tensor_tensor_scan(b[:], k.ones[0:R, :], logf[:], 0.0, ALU.mult, ALU.add).then_inc(dve_row, 1)
            dve.wait_ge(dve_row, 2)
            nc.vector.tensor_tensor(a[:], i_row[:], b[:], ALU.subtract).then_inc(dve_row, 1)
            nc.vector.tensor_copy(ends[:, 1:2], b[:, P - 1:P]).then_inc(dve_row, 1)
            dve.wait_ge(dve_row, 4)
            nc.vector.tensor_reduce(ends[:, 0:1], a[:], AXX, ALU.max).then_inc(dve_row, 1)
            dve.wait_ge(act_new, 3)
            nc.vector.scalar_tensor_tensor(out=new_logf[:], in0=new[:, MLH:G], scalar=0.0, in1=new_soft[:],
                                           op0=ALU.min, op1=ALU.subtract).then_inc(dve_new, 1)
            dve.wait_ge(dve_new, 1)
            nc.vector.tensor_tensor(carried[:], new_logf[:], m_old[:], ALU.add).then_inc(dve_new, 1)
            dve.wait_ge(dve_new, 2)
            nc.vector.tensor_tensor(m_new[:], carried[:], new[:, 0:MLH], ALU.max).then_inc(dve_new, 2)
            dve.wait_ge(dve_new, 4)
            nc.vector.tensor_tensor(new_diff[:, 0, :], new[:, 0:MLH], m_new[:], ALU.subtract).then_inc(dve_new, 1)
            nc.vector.tensor_tensor(new_diff[:, 1, :], carried[:], m_new[:], ALU.subtract).then_inc(dve_new, 1)
            dve.wait_ge(turned, 1)
            nc.vector.tensor_copy(end_rows[:].rearrange("o k r -> o (k r)"), tiny[0:1, 0:2 * R]).then_inc(dve_row, 1)
            dve.wait_ge(dve_row, 6)
            for h in range(MLH):
                rs = slice(h * TB, (h + 1) * TB)
                nc.vector.tensor_tensor_scan(m_row[:, h, 1:TB + 1], end_rows[:, 0, rs], end_rows[:, 1, rs], 0.0,
                                             ALU.max, ALU.add).then_inc(dve_row, 1)
            dve.wait_ge(dve_row, 10)
            nc.vector.tensor_copy(m_prev_row[:].rearrange("o (h c) -> o h c", c=TB),
                                  m_row[:, :, 0:TB]).then_inc(dve_row, 1)
            nc.vector.tensor_tensor_scan(soft[:], a[:], a[:], FAR * 1e4, ALU.max, ALU.max).then_inc(dve_row, 1)
            dve.wait_ge(turned, 2)
            nc.vector.tensor_copy(m_prev[:], tiny[0:R, 3 * R:3 * R + 1]).then_inc(turned, 1)
            dve.wait_ge(turned, 3)
            dve.wait_ge(dve_row, 12)
            nc.vector.tensor_scalar(top[:], soft[:], m_prev[:], None, ALU.max).then_inc(dve_row, 1)
            dve.wait_ge(dve_row, 13)
            nc.vector.tensor_scalar(out_rows[:, 0, :], top[:], -1.0, None, ALU.mult).then_inc(dve_row, 1)
            nc.vector.tensor_tensor(b[:], b[:], top[:], ALU.add).then_inc(dve_row, 1)
            dve.wait_ge(turned, 4)
            nc.vector.tensor_copy(k.a_col[:], k.bank[4][:, 0:R])
            nc.vector.tensor_copy(k.n_old[:].rearrange("p h b -> p b h"),
                                  k.bank[4][:, P:P + R].rearrange("p (b h) -> p b h", h=MLH))

        @block.tensor
        def _(pe):
            proj.projected.credit(pe)
            proj.multiply(pe, 0, 0)
            pe.wait_ge(dve_row, 5)
            nc.tensor.transpose(tiny[0:1, 0:R], ends[:, 0:1], k.ident[0:R, 0:R])
            nc.tensor.transpose(tiny[0:1, R:2 * R], ends[:, 1:2], k.ident[0:R, 0:R]).then_inc(turned, 1)
            pe.wait_ge(dve_row, 11)
            nc.tensor.transpose(tiny[0:R, 3 * R:3 * R + 1], m_prev_row[:], k.ident[0:1, 0:1]).then_inc(turned, 1)
            pe.wait_ge(turned, 3)
            nc.tensor.transpose(k.bank[4][:, 0:R], a[:], k.ident[0:R, 0:R])
            nc.tensor.transpose(k.bank[4][:, P:P + R], n_rows[:], k.ident[0:R, 0:R]).then_inc(turned, 1)


def mlstm(nc, ctx, k):
    sb = lambda name, shape, dt=F32: ctx.enter_context(nc.sbuf_tensor("b_" + name, shape, dt))
    S = lambda name, per, unit=1: Signal(ctx, nc, "b_" + name, per, unit)
    sem = lambda name: nc.alloc_semaphore("b_" + name)
    proj = Projection(ctx, nc, "b", 5, 2, k.xh, k.xl, k.bank[0:3])
    kT, vT, qT, sig = (sb(n, [P, NT]) for n in ("kT", "vT", "qT", "sig"))
    kw_tok, v_tok = sb("kw_tok", [P, TB, P]), sb("v_tok", [P, TB, P + 1])
    rows = sb("rows", [P, 3, T])
    new_rows = sb("new_rows", [P, 3, NB])
    a_col, w_col = sb("a_col_h", [P, TB]), sb("w_col", [P, TB])
    W = sb("W", [P, TB, P])
    qw = sb("qw", [P, TB, P])
    C = sb("C", [P, TB + 1, P + 1])
    n_wide = sb("n_wide", [P, TB, P])
    v_diag = n_wide
    C_old, C_new = sb("C_old", [P, NB, P]), sb("C_new", [P, NB, P])
    k_new, qn = sb("k_new", [P, NB]), sb("qn", [P, NB])
    n_new = sb("n_new", [P, NB + 1])
    n_out = sb("n_out", [NB + 1, P])
    mix = sb("mix", [P, NT])
    den, h, sq = sb("den", [P, NT]), sb("h", [P, NT]), sb("sq", [P, NT])
    gain_all, gain = sb("gain_all", [P, MLH]), sb("gain", [P, 1])
    new_all = sb("new_all", [P, NB, 3 * MLH])
    n_old_h = sb("n_old_h", [P, NB])
    LO, HI, U, TINY = k.bank[3], k.bank[4], k.bank[5:8], k.bank[7]
    quad = lambda bank: bank[:, :].rearrange("p (b t) -> p b t", b=4)
    halves = (LO, HI)
    DEN = (k.bank[5], k.bank[6])

    small_in, sending = sem("small_in"), sem("sending")
    rows_in, C_in = S("rows_in", 1, 16), S("C_in", 1, 16)
    small_set = S("small_set", 4)
    w_arg, w_ready = S("w_arg", 1), S("w_ready", 1)
    turned, tok_taken = S("turned", 4), S("tok_taken", 4)
    scored, W_arg, W_ready, SW_ready = S("scored", 2), S("W_arg", 2), S("W_ready", 2), S("SW_ready", 2)
    updates, C_ready = S("updates", 3), S("C_ready", TB)
    qw_ready, n_wide_ready = S("qw_ready", 1), S("n_wide_ready", 1)
    diag_ready, v_spread = S("diag_ready", 1), S("v_spread", 1)
    k_new_ready, n_new_ready, carried, C_new_ready = S("k_new_ready", 1), S("n_new_ready", 3), S("carried", 1), S("C_new_ready", 1)
    numer, new_numer = S("numer", 2), S("new_numer", 1)
    denom, den_abs, den_ready = S("denom", 1), S("den_abs", 1), S("den_ready", 2)
    den_ln, den_inv = S("den_ln", 1), S("den_inv", 1)
    h_ready, sq_ready, sq_summed, ln_done, rstd_ready = S("h_ready", 4), S("sq_ready", 1), S("sq_summed", 1), S("ln_done", 1), S("rstd_ready", 1)
    normed, mixed = S("normed", 1), S("mixed", 1)
    n_turned, n_kept = S("n_turned", 1), S("n_kept", 1)
    new_kept, mix_out, mix_free = S("new_kept", 1), S("mix_out", 1, 16), S("mix_free", 2)
    out_done, written = S("out_done", 4, 16), S("written", 1)

    with nc.Block() as block:

        @block.sync
        def _(sp):
            sp.dma_start(gain_all[:], k.mlstm_norm, allow_slow_non_contiguous=True).then_inc(small_in, 16)
            sp.dma_start(new_all[:].rearrange("p b r -> p (b r)"), k.new_rows_dram.rearrange("(o b) r -> o (b r)", o=1)
                         .to_broadcast([P, NB * 3 * MLH])).then_inc(small_in, 16)
            written.credit(sp)
            with sp.Fori(0, MLH) as i:
                first = [sp.snap(i * P + base) for base in (B_K, B_V, B_Q, B_O, B_G)]
                proj.load(sp, i, 0, k.w_in[:, :, bass.ds(first[0], P)])
                proj.load(sp, i, 1, k.w_in[:, :, bass.ds(first[1], P)])
                sp.dma_start(rows[:], k.rows_dram.rearrange("k h t -> h k t")[bass.ds(i, 1)]
                             .to_broadcast([P, 3, T])).then_inc(rows_in.sem, 16)
                sp.dma_start(C_old[:], k.state_C[:, :, bass.ds(i, 1), :].rearrange("k b h v -> k b (h v)")).then_inc(C_in.sem, 16)
                for j in (2, 3, 4):
                    proj.load(sp, i, j, k.w_in[:, :, bass.ds(first[j], P)])
                sp.wait_ge(C_ready.sem, C_ready.at(i, TB))
                sp.sem_inc(sending, 1)
                sp.dma_start(k.C_prompt[:, bass.ds(i, 1), :].rearrange("k h v -> k (h v)"), C[:, TB, 0:P]).then_inc(out_done.sem, 16)
                sp.wait_ge(C_new_ready.sem, C_new_ready.at(i, 1))
                sp.sem_inc(sending, 1)
                sp.dma_start(k.C_sample[:, :, bass.ds(i, 1), :].rearrange("k b h v -> k b (h v)"), C_new[:]).then_inc(out_done.sem, 16)
                sp.wait_ge(n_kept.sem, n_kept.at(i, 1))
                sp.sem_inc(sending, 1)
                sp.dma_start(k.n_sample[:, bass.ds(i * P, P)], n_out[0:NB, :]).then_inc(out_done.sem, 16)
                sp.dma_start(k.n_prompt[:, bass.ds(i * P, P)], n_out[NB:NB + 1, :]).then_inc(out_done.sem, 16)
                sp.wait_ge(out_done.sem, out_done.at(i, 4))
                sp.sem_inc(written.sem, 1)

        @block.scalar
        def _(act):
            for s in (proj.hi_ready, proj.taken, w_ready, W_ready, n_wide_ready, den_abs, den_ln, den_inv, sq_ready, ln_done, rstd_ready):
                s.credit(act)
            with act.Fori(0, MLH) as i:
                chunk = lambda dst: lambda c: dst[:, c * CH:(c + 1) * CH]
                load_tables(nc, act, LN_EXP)
                proj.split_hi(act, i, 0)
                proj.split_hi(act, i, 1)
                act.wait_ge(k_new_ready.sem, k_new_ready.at(i, 0))
                proj.take(act, i, 0, chunk(kT), ACT.Copy, scale=DK ** -0.5)
                act.wait_ge(diag_ready.sem, diag_ready.at(i, 0))
                proj.split_hi(act, i, 2)
                proj.take(act, i, 1, chunk(vT), ACT.Copy)
                act.wait_ge(w_arg.sem, w_arg.at(i, 1))
                nc.scalar.activation(w_col[:], w_col[:], ACT.Exp).then_inc(w_ready.sem, 1)
                for q in range(2):
                    act.wait_ge(W_arg.sem, W_arg.at(i, q + 1))
                    nc.scalar.activation(W[:, 4 * q:4 * q + 4, :], W[:, 4 * q:4 * q + 4, :],
                                         ACT.Exp).then_inc(W_ready.sem, 1)
                proj.split_hi(act, i, 3)
                act.wait_ge(new_numer.sem, new_numer.at(i, 0))
                act.wait_ge(qw_ready.sem, qw_ready.at(i, 0))
                act.wait_ge(n_new_ready.sem, n_new_ready.at(i, 0))
                proj.take(act, i, 2, chunk(qT), ACT.Copy)
                proj.split_hi(act, i, 4)
                act.wait_ge(h_ready.sem, h_ready.at(i, 0))
                proj.take(act, i, 3, chunk(sig), ACT.Sigmoid)
                act.wait_ge(C_ready.sem, C_ready.at(i, TB))
                act.wait_ge(v_spread.sem, v_spread.at(i, 1))
                for c in range(TB):
                    last = nc.scalar.activation(n_wide[:, c, :], k.ones[:], ACT.Copy, scale=C[:, c, P:P + 1])
                last.then_inc(n_wide_ready.sem, 1)
                act.wait_ge(denom.sem, denom.at(i, 1))
                for q in range(2):
                    nc.scalar.activation(den[:, 512 * q:512 * q + 512], DEN[q][:, :], ACT.Abs)
                nc.scalar.activation(den[:, T:NT], TINY[:, NB:2 * NB], ACT.Abs).then_inc(den_abs.sem, 1)
                load_tables(nc, act, LN_EXP)
                act.wait_ge(den_ready.sem, den_ready.at(i, 2))
                nc.scalar.activation(den[:], den[:], ACT.Ln).then_inc(den_ln.sem, 1)
                act.wait_ge(den_ln.sem, den_ln.at(i, 1))
                nc.scalar.activation(den[:], den[:], ACT.Exp, scale=-1.0).then_inc(den_inv.sem, 1)
                act.wait_ge(mix_free.sem, mix_free.at(i, 0))
                act.wait_ge(new_kept.sem, new_kept.at(i, 0))
                proj.take(act, i, 4, chunk(mix), ACT.Silu)
                act.wait_ge(h_ready.sem, h_ready.at(i, 4))
                nc.scalar.activation(sq[:], h[:], ACT.Square).then_inc(sq_ready.sem, 1)
                load_tables(nc, act, LN_EXP)
                act.wait_ge(sq_summed.sem, sq_summed.at(i, 1))
                for q in range(2):
                    nc.scalar.activation(den[:, 512 * q:512 * q + 512], halves[q][:, :], ACT.Ln, scale=1.0 / P, bias=k.eps[:])
                nc.scalar.activation(den[:, T:NT], TINY[:, 2 * NB:3 * NB], ACT.Ln, scale=1.0 / P,
                                     bias=k.eps[:]).then_inc(ln_done.sem, 1)
                act.wait_ge(ln_done.sem, ln_done.at(i, 1))
                nc.scalar.activation(sq[:], den[:], ACT.Exp, scale=-0.5).then_inc(rstd_ready.sem, 1)

        @block.vector
        def _(dve):
            for s in (proj.lo_ready, small_set, w_arg, tok_taken, W_arg, SW_ready, C_ready, qw_ready, diag_ready,
                      k_new_ready, n_new_ready, carried, C_new_ready, den_ready, h_ready, normed, mixed, n_kept, new_kept):
                s.credit(dve)
            nc.vector.memset(C[:, 0, :], 0.0)
            nc.vector.memset(v_tok[:, :, P:P + 1], 1.0)
            dve.wait_ge(small_in, 32)
            with dve.Fori(0, MLH) as i:
                proj.split_lo(dve, i, 0)
                proj.split_lo(dve, i, 1)
                nc.vector.tensor_copy(gain[:], gain_all[:, bass.ds(i, 1)]).then_inc(small_set.sem, 1)
                nc.vector.tensor_copy(a_col[:], k.a_col[:, bass.ds(i * TB, TB)]).then_inc(small_set.sem, 1)
                nc.vector.tensor_copy(n_old_h[:], k.n_old[:, bass.ds(i, 1), :]
                                      .rearrange("p a b -> p (a b)")).then_inc(small_set.sem, 1)
                nc.vector.tensor_copy(new_rows[:], new_all[:].rearrange("p b (k h) -> p h k b", h=MLH)[:, bass.ds(i, 1)]
                                      .rearrange("p a k b -> p (a k) b")).then_inc(small_set.sem, 1)
                dve.wait_ge(small_set.sem, small_set.at(i, 4))
                dve.wait_ge(rows_in.sem, rows_in.at(i, 1))
                ends = rows[:, 0, :].rearrange("p (c t) -> p c t", t=P)[:, :, P - 1:P].rearrange("p c t -> p (c t)")
                nc.vector.tensor_tensor(w_col[:], a_col[:], ends, ALU.add).then_inc(w_arg.sem, 1)
                for q in range(2):
                    for c in range(4 * q, 4 * q + 4):
                        last = nc.vector.scalar_tensor_tensor(out=W[:, c, :], in0=rows[:, 0, c * P:(c + 1) * P],
                                                              scalar=a_col[:, c:c + 1], in1=k.up_to[:],
                                                              op0=ALU.add, op1=ALU.min)
                    last.then_inc(W_arg.sem, 1)
                dve.wait_ge(w_ready.sem, w_ready.at(i, 1))
                for q in range(2):
                    dve.wait_ge(turned.sem, turned.at(i, q + 1))
                    w = w_col[:, 4 * q:4 * q + 4].rearrange("p (c o) -> p c o", o=1).to_broadcast([P, 4, P])
                    nc.vector.tensor_tensor(kw_tok[:, 4 * q:4 * q + 4, :], quad(halves[q]), w,
                                            ALU.mult).then_inc(tok_taken.sem, 1)
                proj.split_lo(dve, i, 2)
                for q in range(2):
                    dve.wait_ge(turned.sem, turned.at(i, q + 3))
                    nc.vector.tensor_copy(v_tok[:, 4 * q:4 * q + 4, 0:P], quad(halves[q])).then_inc(tok_taken.sem, 1)
                for b in range(NB):
                    last = nc.vector.tensor_scalar(v_diag[:, b, :], k.ident[:], vT[:, T + b:T + b + 1], None, ALU.mult)
                last.then_inc(diag_ready.sem, 1)
                nc.vector.tensor_tensor(k_new[:], kT[:, T:NT], new_rows[:, 0, :], ALU.mult).then_inc(k_new_ready.sem, 1)
                dve.wait_ge(k_new_ready.sem, k_new_ready.at(i, 1))
                nc.vector.tensor_tensor(n_new[:, 0:NB], n_old_h[:], new_rows[:, 1, :], ALU.mult).then_inc(n_new_ready.sem, 1)
                dve.wait_ge(n_new_ready.sem, n_new_ready.at(i, 1))
                nc.vector.tensor_tensor(n_new[:, 0:NB], n_new[:, 0:NB], k_new[:], ALU.add).then_inc(n_new_ready.sem, 1)
                proj.split_lo(dve, i, 3)
                dve.wait_ge(written.sem, written.at(i, 0))
                for c in range(TB):
                    dve.wait_ge(updates.sem, updates.at(i, c // 3 + 1))
                    dve.wait_ge(C_ready.sem, C_ready.at(i, c))
                    nc.vector.scalar_tensor_tensor(out=C[:, c + 1, :], in0=C[:, c, :],
                                                   scalar=rows[:, 1, c * P + P - 1:c * P + P],
                                                   in1=U[c // 3][:, (c % 3) * (P + 1):(c % 3 + 1) * (P + 1)],
                                                   op0=ALU.mult, op1=ALU.add).then_inc(C_ready.sem, 1)
                for q in range(2):
                    dve.wait_ge(scored.sem, scored.at(i, q + 1))
                    dve.wait_ge(W_ready.sem, W_ready.at(i, q + 1))
                    nc.vector.tensor_tensor(W[:, 4 * q:4 * q + 4, :], quad(halves[q]), W[:, 4 * q:4 * q + 4, :],
                                            ALU.mult).then_inc(SW_ready.sem, 1)
                nc.vector.tensor_tensor(qw[:].rearrange("p c t -> p (c t)"), qT[:, 0:T], rows[:, 1, :],
                                        ALU.mult).then_inc(qw_ready.sem, 1)
                dve.wait_ge(C_ready.sem, C_ready.at(i, TB))
                dve.wait_ge(n_new_ready.sem, n_new_ready.at(i, 2))
                nc.vector.tensor_copy(n_new[:, NB:NB + 1], C[:, TB, P:P + 1])
                nc.vector.tensor_tensor(qn[:], n_new[:, 0:NB], qT[:, T:NT], ALU.mult).then_inc(n_new_ready.sem, 1)
                dve.wait_ge(C_in.sem, C_in.at(i, 1))
                wide = new_rows[:, 1, :].rearrange("p (b o) -> p b o", o=1).to_broadcast([P, NB, P])
                nc.vector.tensor_tensor(C_old[:], C_old[:], wide, ALU.mult).then_inc(carried.sem, 1)
                proj.split_lo(dve, i, 4)
                dve.wait_ge(carried.sem, carried.at(i, 1))
                dve.wait_ge(v_spread.sem, v_spread.at(i, 1))
                for b in range(NB):
                    last = nc.vector.scalar_tensor_tensor(out=C_new[:, b, :], in0=quad(DEN[b // 4])[:, b % 4, :],
                                                          scalar=k_new[:, b:b + 1], in1=C_old[:, b, :],
                                                          op0=ALU.mult, op1=ALU.add)
                last.then_inc(C_new_ready.sem, 1)
                dve.wait_ge(den_abs.sem, den_abs.at(i, 1))
                nc.vector.tensor_tensor(den[:, 0:T], den[:, 0:T], rows[:, 2, :], ALU.max).then_inc(den_ready.sem, 1)
                nc.vector.tensor_tensor(den[:, T:NT], den[:, T:NT], new_rows[:, 2, :], ALU.max).then_inc(den_ready.sem, 1)
                dve.wait_ge(den_inv.sem, den_inv.at(i, 1))
                dve.wait_ge(n_turned.sem, n_turned.at(i, 1))
                nc.vector.tensor_tensor(h[:, T:NT], TINY[:, 0:NB], den[:, T:NT], ALU.mult).then_inc(h_ready.sem, 1)
                nc.vector.tensor_copy(n_out[:], TINY[0:NB + 1, P:2 * P]).then_inc(n_kept.sem, 1)
                for q in range(2):
                    nc.vector.tensor_tensor(h[:, 512 * q:512 * q + 512], halves[q][:, :], den[:, 512 * q:512 * q + 512],
                                            ALU.mult).then_inc(h_ready.sem, 1)
                dve.wait_ge(h_ready.sem, h_ready.at(i, 3))
                dve.wait_ge(proj.taken.sem, proj.taken.at(i, 15))
                nc.vector.tensor_tensor(h[:], h[:], sig[:], ALU.mult).then_inc(h_ready.sem, 1)
                dve.wait_ge(h_ready.sem, h_ready.at(i, 4))
                dve.wait_ge(rstd_ready.sem, rstd_ready.at(i, 1))
                nc.vector.scalar_tensor_tensor(out=sq[:], in0=h[:], scalar=gain[:], in1=sq[:],
                                               op0=ALU.mult, op1=ALU.mult).then_inc(normed.sem, 1)
                dve.wait_ge(normed.sem, normed.at(i, 1))
                nc.vector.tensor_tensor(mix[:], mix[:], sq[:], ALU.mult).then_inc(mixed.sem, 1)
                dve.wait_ge(mixed.sem, mixed.at(i, 1))
                nc.vector.tensor_copy(k.new_mix[:, bass.ds(i + GT, 1), :].rearrange("p a b -> p (a b)"),
                                      mix[:, T:NT]).then_inc(new_kept.sem, 1)

        @block.gpsimd
        def _(pool):
            mix_free.credit(pool)
            with pool.Fori(0, MLH) as i:
                pool.wait_ge(mixed.sem, mixed.at(i, 1))
                store_mix(nc, pool, k, i + GT, mix, mix_out, i, mix_free)

        @block.tensor
        def _(pe):
            for s in (proj.projected, turned, scored, updates, v_spread, numer, new_numer, denom, sq_summed, n_turned):
                s.credit(pe)
            with pe.Fori(0, MLH) as i:
                def turn(src, first_wait, done):
                    for q in range(2):
                        if done:
                            pe.wait_ge(tok_taken.sem, tok_taken.at(i, q + 1))
                        for b in range(4):
                            last = nc.tensor.transpose(quad(halves[q])[:, b, :], src[:, (4 * q + b) * P:(4 * q + b + 1) * P],
                                                       k.ident[:])
                        last.then_inc(turned.sem, 1)

                proj.multiply(pe, i, 0)
                proj.multiply(pe, i, 1)
                pe.wait_ge(rstd_ready.sem, rstd_ready.at(i, 0))
                turn(kT, 3, False)
                pe.wait_ge(proj.taken.sem, proj.taken.at(i, 6))
                turn(vT, 6, True)
                proj.multiply(pe, i, 2)
                for c in range(TB):
                    if c == 0:
                        pe.wait_ge(tok_taken.sem, tok_taken.at(i, 4))
                        pe.wait_ge(n_kept.sem, n_kept.at(i, 0))
                    last = nc.tensor.matmul(U[c // 3][:, (c % 3) * (P + 1):(c % 3 + 1) * (P + 1)], kw_tok[:, c, :],
                                            v_tok[:, c, :], start=True, stop=True)
                    if c % 3 == 2 or c == TB - 1:
                        last.then_inc(updates.sem, 1)
                pe.wait_ge(proj.taken.sem, proj.taken.at(i, 9))
                for c in range(TB):
                    last = nc.tensor.matmul(quad(halves[c // 4])[:, c % 4, :], kT[:, c * P:(c + 1) * P],
                                            qT[:, c * P:(c + 1) * P], start=True, stop=True)
                    if c % 4 == 3:
                        last.then_inc(scored.sem, 1)
                pe.wait_ge(C_ready.sem, C_ready.at(i, TB))
                for q in range(2):
                    last = nc.tensor.matmul(DEN[q][:, :], k.ones[:], v_diag[:, 4 * q:4 * q + 4, :]
                                            .rearrange("p b v -> p (b v)"), start=True, stop=True)
                last.then_inc(v_spread.sem, 1)
                proj.multiply(pe, i, 3)
                for q in range(2):
                    pe.wait_ge(SW_ready.sem, SW_ready.at(i, q + 1))
                    if q == 0:
                        pe.wait_ge(qw_ready.sem, qw_ready.at(i, 1))
                    for c in range(4 * q, 4 * q + 4):
                        nc.tensor.matmul(quad(halves[q])[:, c % 4, :], v_tok[:, c, 0:P], W[:, c, :], start=True, stop=False)
                        last = nc.tensor.matmul(quad(halves[q])[:, c % 4, :], C[:, c, 0:P], qw[:, c, :],
                                                start=False, stop=True)
                    last.then_inc(numer.sem, 1)
                pe.wait_ge(C_new_ready.sem, C_new_ready.at(i, 1))
                for b in range(NB):
                    last = nc.tensor.matmul(TINY[:, b:b + 1], C_new[:, b, :], qT[:, T + b:T + b + 1], start=True, stop=True)
                last.then_inc(new_numer.sem, 1)
                pe.wait_ge(n_new_ready.sem, n_new_ready.at(i, 3))
                nc.tensor.matmul(TINY[:, NB:2 * NB], k.ones[:], qn[:], start=True, stop=True)
                nc.tensor.transpose(TINY[0:NB + 1, P:2 * P], n_new[:], k.ident[:]).then_inc(n_turned.sem, 1)
                pe.wait_ge(n_wide_ready.sem, n_wide_ready.at(i, 1))
                for c in range(TB):
                    q = c // 4
                    nc.tensor.matmul(quad(DEN[q])[:, c % 4, :], k.ones[:], W[:, c, :], start=True, stop=False)
                    last = nc.tensor.matmul(quad(DEN[q])[:, c % 4, :], n_wide[:, c, :], qw[:, c, :], start=False, stop=True)
                last.then_inc(denom.sem, 1)
                proj.multiply(pe, i, 4)
                pe.wait_ge(sq_ready.sem, sq_ready.at(i, 1))
                for q in range(2):
                    nc.tensor.matmul(halves[q][:, :], k.ones[:], sq[:, 512 * q:512 * q + 512], start=True, stop=True)
                nc.tensor.matmul(TINY[:, 2 * NB:3 * NB], k.ones[:], sq[:, T:NT], start=True,
                                 stop=True).then_inc(sq_summed.sem, 1)


def new_queries(nc, ctx, k):
    sb = lambda name, shape, dt=F32: ctx.enter_context(nc.sbuf_tensor("q_" + name, shape, dt))
    sem = lambda name: nc.alloc_semaphore("q_" + name)
    w, x_new = sb("w", [P, KT, GW]), sb("x_new", [P, KT, NB])
    partial, rows = sb("partial", [P, GW]), sb("rows", [NB, GW])
    w_in, ready, added, copied, folded, scaled, out = (sem(n) for n in ("w_in", "ready", "added", "copied", "folded", "scaled", "out"))
    SUM, FOLDED = k.bank[0], k.bank[1]
    with nc.Block() as block:

        @block.sync
        def _(sp):
            sp.dma_start(w[:], k.w_in[:, :, C_Q:C_Q + GW]).then_inc(w_in, 16)
            sp.wait_ge(scaled, 1)
            sp.dma_start(k.q_dram, rows[:]).then_inc(out, 16)
            sp.wait_ge(out, 16)

        @block.vector
        def _(dve):
            nc.vector.memset(SUM[:, :], 0.0).then_inc(ready, 1)
            nc.vector.tensor_tensor(x_new[:], k.xh[:, :, T:NT].bitcast(F32), k.xl[:, :, T:NT].bitcast(F32),
                                    ALU.add).then_inc(ready, 1)
            dve.wait_ge(added, 1)
            nc.vector.tensor_copy(partial[:], SUM[:, :]).then_inc(copied, 1)
            dve.wait_ge(folded, 1)
            nc.vector.tensor_scalar(rows[:], FOLDED[0:NB, :], SCORE_SCALE, None, ALU.mult).then_inc(scaled, 1)

        @block.tensor
        def _(pe):
            pe.wait_ge(ready, 2)
            pe.wait_ge(w_in, 16)
            for kk in range(KT):
                g = 32 * (kk % 4)
                last = nc.tensor.matmul(SUM[g:g + NB, :], x_new[:, kk, :], w[:, kk, :], start=(kk < 4), stop=(kk >= 4),
                                        skip_group_check=True)
            last.then_inc(added, 1)
            pe.wait_ge(copied, 1)
            nc.tensor.matmul(FOLDED[0:NB, :], k.fold[:], partial[:], start=True, stop=True).then_inc(folded, 1)


class PagedAttention:

    PAIRS = NPG // 2

    def __init__(self, ctx, nc, k, tag, first, count, ring, sums, partial, folded, gathered):
        sb = lambda name, shape, dt=F32: ctx.enter_context(nc.sbuf_tensor(f"{tag}_{name}", shape, dt))
        S = lambda name, per, unit=1: Signal(ctx, nc, f"{tag}_{name}", per, unit)
        self.nc, self.k, self.first, self.count, self.ring = nc, k, first, count, ring
        self.SUMS, self.PARTIAL, self.FOLDED, self.GATHERED = sums, partial, folded, gathered
        self.keys, self.values = sb("keys", [P, ring, 2, GW]), sb("values", [P, ring, 2, GW])
        self.page_ids, self.bias, self.q = sb("page_ids", [1, NB * NPG], I32), sb("page_bias", [P, SBH]), sb("q", [P, GW])
        self.z, self.soft, self.L, self.total, self.inclusive = (sb("page_" + n, [P, SBH, NPG])
                                                                 for n in ("z", "soft", "L", "total", "inclusive"))
        self.A = sb("page_A", [P, NPG, SBH])
        self.y_rows, self.y_own = sb("y_rows", [P, count, GW]), sb("y_own", [SBH, GW])
        self.own = sb("own", [SBH, GW])
        self.one8 = sb("one8", [SBH, 1])
        sem = lambda name: nc.alloc_semaphore(f"{tag}_{name}")
        self.loaded, self.tables, self.cleared = sem("page_loaded"), sem("page_tables"), sem("page_cleared")
        self.sending, self.multiplying = sem("page_sending"), sem("page_multiplying")
        NP = self.PAIRS
        self.q_in = S("q_in", 1, 16)
        self.K_in = [S(f"keys_in{s}", 2 * NP // ring, 16) for s in range(ring)]
        self.V_in = [S(f"values_in{s}", 2 * NP // ring, 16) for s in range(ring)]
        self.scaled, self.z_ready, self.biased = S("scaled", NP), S("z_ready", NP), S("biased", 1)
        self.abs_done, self.exp_done, self.ln_done = S("page_abs", 1), S("page_exp", 1), S("page_ln", 1)
        self.L_ready, self.summed, self.total_taken = S("page_L_ready", 1), S("page_summed", 1), S("total_taken", 1)
        self.scanned, self.x_ready, self.A_ready = S("scanned", SBH), S("page_x_ready", 2), S("page_A_ready", 1)
        self.weighed, self.rows_taken, self.fold_done = S("weighed", NP), S("rows_taken", 1), S("fold_done", 1)
        self.own_ready, self.gather_done, self.kept = S("own_ready", 1), S("gather_done", 1), S("y_kept", 1)

    def setup_sync(self, sp):
        sp.dma_start(self.page_ids[:], self.k.page_table.rearrange("(o b) p -> o (b p)", o=1)).then_inc(self.loaded, 16)
        sp.dma_start(self.bias[:], self.k.sb_logit_bias.to_broadcast([P, SBH])).then_inc(self.loaded, 16)
        sp.wait_ge(self.loaded, 32)

    def setup_pool(self, pool):
        nc, own = self.nc, self.own
        self.scaled.credit(pool)
        nc.gpsimd.memset(own[:], 1.0).then_inc(self.tables, 1)
        nc.gpsimd.memset(self.one8[:], 1.0).then_inc(self.tables, 1)
        pool.wait_ge(self.tables, 2)
        nc.gpsimd.affine_select(out=own[:], in_=own[:], compare_op=ALU.is_ge, fill=0.0, base=0,
                                pattern=[[1, GW]], channel_multiplier=-SBD).then_inc(self.tables, 1)
        pool.wait_ge(self.tables, 3)
        nc.gpsimd.affine_select(out=own[:], in_=own[:], compare_op=ALU.is_ge, fill=0.0, base=SBD - 1,
                                pattern=[[-1, GW]], channel_multiplier=SBD).then_inc(self.tables, 1)

    def setup_vector(self, dve):
        for s in (self.z_ready, self.biased, self.L_ready, self.total_taken, self.scanned, self.x_ready,
                  self.rows_taken, self.own_ready, self.kept):
            s.credit(dve)
        self.nc.vector.memset(self.PARTIAL[:, :], 0.0).then_inc(self.cleared, 1)
        dve.wait_ge(self.loaded, 32)
        dve.wait_ge(self.tables, 4)

    def setup_scalar(self, act):
        for s in (self.abs_done, self.exp_done, self.ln_done, self.A_ready):
            s.credit(act)

    def setup_tensor(self, pe):
        for s in (self.summed, self.weighed, self.fold_done, self.gather_done):
            s.credit(pe)
        pe.wait_ge(self.tables, 4)
        pe.wait_ge(self.cleared, 1)

    def load_query(self, queue, i):
        queue.wait_ge(self.scaled.sem, self.scaled.at(i, 0))
        queue.sem_inc(self.sending, 1)
        queue.dma_start(self.q[:], self.k.q_dram[bass.ds(i + self.first, 1), :].to_broadcast([P, GW]))\
            .then_inc(self.q_in.sem, 16)

    def load_pair(self, queue, i, r, s, ring, cache, landed, freed):
        pages = [queue.value_load(self.page_ids[0:1, bass.ds((i + self.first) * NPG - 2 * r + (NPG - 1 - e), 1)],
                                  min_val=0, max_val=self.k.n_phys - 1) for e in range(2)]
        queue.wait_ge(freed.sem, freed.at(i, r - self.ring + 1))
        queue.sem_inc(self.sending, 1)
        for e in range(2):
            queue.dma_start(ring[:, s, e, :], cache[bass.ds(pages[e] * PAGE, PAGE), :]).then_inc(landed[s].sem, 16)

    def load_keys(self, queue, i, r):
        self.load_pair(queue, i, r, r % self.ring, self.keys, self.k.cache_k, self.K_in, self.z_ready)

    def load_values(self, queue, i, r):
        self.load_pair(queue, i, r, r % self.ring, self.values, self.k.cache_v, self.V_in, self.weighed)

    def load_all_values(self, queue, i):
        with queue.Fori(0, self.PAIRS // self.ring) as turn:
            for s in range(self.ring):
                self.load_pair(queue, i, turn * self.ring + s, s, self.values, self.k.cache_v, self.V_in, self.weighed)

    def multiply_keys(self, pool, i, r):
        s = r % self.ring
        if r == 0:
            pool.wait_ge(self.q_in.sem, self.q_in.at(i, 1))
        pool.wait_ge(self.K_in[s].sem, self.K_in[s].at(i, 2 * (r // self.ring + 1)))
        q = self.q[:].rearrange("p (o c) -> p o c", o=1).to_broadcast([P, 2, GW])
        self.nc.gpsimd.tensor_tensor(self.keys[:, s], self.keys[:, s], q, ALU.mult).then_inc(self.scaled.sem, 1)

    def reduce_keys(self, dve, i, r):
        if r == 0:
            dve.wait_ge(self.A_ready.sem, self.A_ready.at(i, 0))
        dve.wait_ge(self.scaled.sem, self.scaled.at(i, r + 1))
        self.nc.vector.tensor_reduce(self.z[:, :, 2 * r:2 * r + 2].rearrange("p h r -> p r h"),
                                     self.keys[:, r % self.ring].rearrange("p r (h d) -> p r h d", d=SBD), AXX,
                                     ALU.add).then_inc(self.z_ready.sem, 1)

    def add_bias(self, dve, i):
        dve.wait_ge(self.z_ready.sem, self.z_ready.at(i, self.PAIRS))
        wide = self.bias[:].rearrange("p (h o) -> p h o", o=1).to_broadcast([P, SBH, NPG])
        self.nc.vector.tensor_tensor(self.z[:], self.z[:], wide, ALU.add).then_inc(self.biased.sem, 1)

    def softplus_tail(self, act, i):
        nc, soft = self.nc, self.soft
        act.wait_ge(self.biased.sem, self.biased.at(i, 1))
        nc.scalar.activation(soft[:], self.z[:], ACT.Abs).then_inc(self.abs_done.sem, 1)
        act.wait_ge(self.abs_done.sem, self.abs_done.at(i, 1))
        nc.scalar.activation(soft[:], soft[:], ACT.Exp, scale=-1.0).then_inc(self.exp_done.sem, 1)
        act.wait_ge(self.exp_done.sem, self.exp_done.at(i, 1))
        nc.scalar.activation(soft[:], soft[:], ACT.Ln, bias=1.0).then_inc(self.ln_done.sem, 1)

    def softplus(self, dve, i):
        dve.wait_ge(self.ln_done.sem, self.ln_done.at(i, 1))
        self.nc.vector.scalar_tensor_tensor(out=self.L[:], in0=self.z[:], scalar=0.0, in1=self.soft[:], op0=ALU.max,
                                            op1=ALU.add).then_inc(self.L_ready.sem, 1)

    def sum_pages(self, pe, i):
        pe.wait_ge(self.L_ready.sem, self.L_ready.at(i, 1))
        flat, HP = self.L[:].rearrange("p h r -> p (h r)"), SBH * NPG
        self.nc.tensor.matmul(self.SUMS[:, 0:HP], self.k.from_here[:], flat, start=True, stop=True)
        self.nc.tensor.matmul(self.SUMS[:, HP:2 * HP], self.k.ones[:], flat, start=True, stop=True).then_inc(self.summed.sem, 1)

    def exponents(self, dve, i):
        nc, z, HP = self.nc, self.z, SBH * NPG
        flat = z[:].rearrange("p h r -> p (h r)")
        dve.wait_ge(self.summed.sem, self.summed.at(i, 1))
        nc.vector.tensor_copy(self.total[:].rearrange("p h r -> p (h r)"), self.SUMS[:, HP:2 * HP]).then_inc(self.total_taken.sem, 1)
        nc.vector.tensor_tensor(flat, flat, self.SUMS[:, 0:HP], ALU.subtract).then_inc(self.x_ready.sem, 1)
        dve.wait_ge(self.total_taken.sem, self.total_taken.at(i, 1))
        for h in range(SBH):
            nc.vector.tensor_tensor_scan(self.inclusive[:, h, :], self.k.ones[:, 0:NPG], self.total[:, h, :], 0.0,
                                         ALU.mult, ALU.add).then_inc(self.scanned.sem, 1)
        dve.wait_ge(self.scanned.sem, self.scanned.at(i, SBH))
        dve.wait_ge(self.x_ready.sem, self.x_ready.at(i, 1))
        nc.vector.tensor_tensor(z[:, :, 1:NPG], z[:, :, 1:NPG], self.inclusive[:, :, 0:NPG - 1],
                                ALU.subtract).then_inc(self.x_ready.sem, 1)

    def weights(self, act, i):
        act.wait_ge(self.x_ready.sem, self.x_ready.at(i, 2))
        act.wait_ge(self.weighed.sem, self.weighed.at(i, 0))
        self.nc.scalar.activation(self.A[:].rearrange("p r h -> p h r"), self.z[:], ACT.Exp).then_inc(self.A_ready.sem, 1)

    def weigh(self, pe, i, r):
        s = r % self.ring
        if r == 0:
            pe.wait_ge(self.A_ready.sem, self.A_ready.at(i, 1))
            pe.wait_ge(self.rows_taken.sem, self.rows_taken.at(i, 0))
        pe.wait_ge(self.V_in[s].sem, self.V_in[s].at(i, 2 * (r // self.ring + 1)))
        for e in range(2):
            p = 2 * r + e
            g = 32 * (p % 4)
            last = self.nc.tensor.matmul(self.PARTIAL[g:g + SBH, :], self.A[:, p, :], self.values[:, s, e, :], start=(p < 4),
                                         stop=(p >= NPG - 4), skip_group_check=True)
        last.then_inc(self.weighed.sem, 1)

    def take_partial(self, dve, i):
        dve.wait_ge(self.weighed.sem, self.weighed.at(i, self.PAIRS))
        self.nc.vector.tensor_copy(self.y_rows[:, bass.ds(i, 1), :].rearrange("p a c -> p (a c)"),
                                   self.PARTIAL[:, :]).then_inc(self.rows_taken.sem, 1)

    def result_tensor(self, pe):
        for i in range(self.count):
            self.fold(pe, i)
            self.gather(pe, i)

    def result_vector(self, dve):
        for i in range(self.count):
            self.own_columns(dve, i)
            self.keep(dve, i)

    def fold(self, pe, i):
        pe.wait_ge(self.rows_taken.sem, self.rows_taken.at(i, 1))
        self.nc.tensor.matmul(self.FOLDED[0:SBH, :], self.k.fold[:], self.y_rows[:, i, :], start=True, stop=True)\
            .then_inc(self.fold_done.sem, 1)

    def own_columns(self, dve, i):
        dve.wait_ge(self.fold_done.sem, self.fold_done.at(i, 1))
        dve.wait_ge(self.gather_done.sem, self.gather_done.at(i, 0))
        self.nc.vector.tensor_tensor(self.y_own[:], self.FOLDED[0:SBH, :], self.own[:], ALU.mult).then_inc(self.own_ready.sem, 1)

    def gather(self, pe, i):
        pe.wait_ge(self.own_ready.sem, self.own_ready.at(i, 1))
        pe.wait_ge(self.kept.sem, self.kept.at(i, 0))
        for g in range(GT):
            last = self.nc.tensor.matmul(self.GATHERED[:, g:g + 1], self.y_own[:, g * P:(g + 1) * P], self.one8[:],
                                         start=True, stop=True)
        last.then_inc(self.gather_done.sem, 1)

    def keep(self, dve, i):
        dve.wait_ge(self.gather_done.sem, self.gather_done.at(i, 1))
        self.nc.vector.tensor_copy(self.k.y_new[:, :, i + self.first],
                                   self.GATHERED[:, 0:GT]).then_inc(self.kept.sem, 1)


def stick_breaking_new(nc, ctx, k):
    first = GT
    a = PagedAttention(ctx, nc, k, "p", first, NB - first, 4, k.bank[0], k.bank[1], k.bank[2], k.bank[3])
    count = NB - first
    NP = a.PAIRS
    with nc.Block() as block:

        @block.sync
        def _(sp):
            a.setup_sync(sp)
            with sp.Fori(0, count) as i:
                a.load_query(sp, i)
                for r in range(NP):
                    a.load_keys(sp, i, r)

        @block.gpsimd
        def _(pool):
            a.setup_pool(pool)
            with pool.Fori(0, count) as i:
                for r in range(NP):
                    a.multiply_keys(pool, i, r)

        @block.scalar
        def _(act):
            a.setup_scalar(act)
            load_tables(nc, act, LN_EXP)
            act.wait_ge(a.loaded, 32)
            with act.Fori(0, count) as i:
                for r in range(a.ring):
                    a.load_values(act, i, r)
                a.softplus_tail(act, i)
                a.weights(act, i)
                for r in range(a.ring, NP):
                    a.load_values(act, i, r)

        @block.vector
        def _(dve):
            a.setup_vector(dve)

            def scores(i):
                for r in range(NP):
                    a.reduce_keys(dve, i, r)

            def attention(i):
                a.add_bias(dve, i)
                a.softplus(dve, i)
                a.exponents(dve, i)

            scores(0)
            with dve.Fori(0, count - 1) as i:
                attention(i)
                scores(i + 1)
                a.take_partial(dve, i)
            attention(count - 1)
            a.take_partial(dve, count - 1)
            a.result_vector(dve)
            dve.wait_ge(a.kept.sem, a.kept.at(count - 1, 1))
            gated = k.new_mix[:, 2 * GT:3 * GT, :]
            nc.vector.tensor_tensor(gated, gated, k.y_new[:], ALU.mult)

        @block.tensor
        def _(pe):
            a.setup_tensor(pe)
            with pe.Fori(0, count) as i:
                pe.wait_ge(a.x_ready.sem, a.x_ready.at(i, 0))
                a.sum_pages(pe, i)
                for r in range(NP):
                    a.weigh(pe, i, r)
            a.result_tensor(pe)


def output(nc, ctx, k):
    sb = lambda name, shape, dt=F32: ctx.enter_context(nc.sbuf_tensor("o_" + name, shape, dt))
    S = lambda name, per, unit=1: Signal(ctx, nc, "o_" + name, per, unit)
    sem = lambda name: nc.alloc_semaphore("o_" + name)
    H = DM // 2
    KO = 4 * GT
    WC = 2
    NW = KO // WC
    w_hi, w_lo = sb("w_hi", [P, KO, DM], F32R), sb("w_lo", [P, KO, DM], F32R)
    raw = sb("raw", [P, WC, DM])
    x = raw
    mix = sb("mix", [P, KO, P])
    hi, lo = sb("mix_hi", [P, 2, KO, P], F32R), sb("mix_lo", [P, 2, KO, P], F32R)
    gain, tmp, junk, new_rows = sb("gain", [P, DM]), sb("tmp", [P, H]), sb("junk", [P, H]), sb("new_rows", [P, H])
    sq, ln, rstd = sb("sq", [P, 2, 2]), sb("ln", [P, 2]), sb("rstd", [P, 2])
    both = sb("both", [P, 2])
    new_sq, new_stat = sb("new_sq", [NB, 2]), sb("new_stat", [NB, 3])
    new_x, new_tmp = sb("new_x", [NB, DM]), sb("new_tmp", [NB, H])
    gain_in, cleared, new_x_in, new_out, sending = sem("gain_in"), sem("cleared"), sem("new_x_in"), sem("new_out"), sem("sending")
    w_in, w_hi_ready, w_lo_ready, new_added = sem("w_in"), sem("w_hi_ready"), sem("w_lo_ready"), sem("new_added")
    mix_in = S("mix_in", 2, 16)
    hi_ready, lo_ready, done = S("hi_ready", 2), S("lo_ready", 2), S("done", 2)
    squared, sums_ready, ln_done, rstd_done = S("squared", 4), S("sums_ready", 2), S("ln_done", 2), S("rstd_done", 2)
    scaled, added = S("scaled", 4), S("added", 4)
    x_in, y_out = [S(f"x_in{b}", 1, 16) for b in range(2)], [S(f"y_out{b}", 1, 16) for b in range(2)]
    new_step, new_folded, new_act = sem("new_step"), sem("new_folded"), sem("new_act")
    ACC = [k.bank[2 * b:2 * b + 2] for b in range(2)]
    NEW, FOLDED = k.bank[4:6], k.bank[6:8]

    with nc.Block() as block:

        @block.sync
        def _(sp):
            sp.dma_start(mix[:], k.mix_dram[:, :, 0:P].rearrange("k p t -> p k t")).then_inc(mix_in.sem, 16)
            for n in range(NW):
                if n >= 1:
                    sp.wait_ge(w_hi_ready, n)
                    sp.wait_ge(w_lo_ready, n)
                    sp.wait_ge(new_added, n)
                sp.dma_start(raw[:], k.w_out[:, WC * n:WC * n + WC, :]).then_inc(w_in, 16)
                if n == 0:
                    sp.wait_ge(hi_ready.sem, hi_ready.at(0, 1))
                    sp.wait_ge(lo_ready.sem, lo_ready.at(0, 1))
                    sp.dma_start(mix[:], k.mix_dram[:, :, P:2 * P].rearrange("k p t -> p k t")).then_inc(mix_in.sem, 16)
                    sp.dma_start(gain[:], k.norm_post.to_broadcast([P, DM])).then_inc(gain_in, 16)
                    sp.dma_start(new_x[:], k.x_sample).then_inc(new_x_in, 16)
            sp.wait_ge(w_hi_ready, NW)
            sp.wait_ge(w_lo_ready, NW)
            sp.wait_ge(new_added, NW)
            def exchange(i):
                for b in range(2):
                    n = i * 2 + b
                    sp.dma_start(x[:, b, :], k.x_by_block[:, bass.ds(n, 1), :].rearrange("p a d -> p (a d)")).then_inc(x_in[b].sem, 16)
                for b in range(2):
                    n = i * 2 + b
                    if not isinstance(i, int) or i < TB // 2 - 1:
                        sp.wait_ge(hi_ready.sem, hi_ready.at(i + 1, b))
                        sp.wait_ge(lo_ready.sem, lo_ready.at(i + 1, b))
                        sp.sem_inc(sending, 1)
                        sp.dma_start(mix[:], k.mix_dram[:, :, bass.ds((n + 2) * P, P)].rearrange("k p t -> p k t")).then_inc(mix_in.sem, 16)
                for b in range(2):
                    n = i * 2 + b
                    sp.wait_ge(added.sem, added.at(i, 2 * b + 2))
                    sp.sem_inc(sending, 1)
                    sp.dma_start(k.y_by_block[:, bass.ds(n, 1), :].rearrange("p a d -> p (a d)"), x[:, b, :]).then_inc(y_out[b].sem, 16)
                for b in range(2):
                    sp.wait_ge(y_out[b].sem, y_out[b].at(i, 1))
                    sp.sem_inc(sending, 1)

            with sp.Fori(0, TB // 2 - 1) as i:
                exchange(i)
            exchange(TB // 2 - 1)
            sp.wait_ge(new_step, 7)
            sp.dma_start(k.y_sample, new_x[:]).then_inc(new_out, 16)
            sp.wait_ge(new_out, 16)

        @block.scalar
        def _(act):
            for s in (hi_ready, squared, ln_done, rstd_done):
                s.credit(act)
            load_tables(nc, act, LN_EXP)

            def split_mix(i, b):
                act.wait_ge(mix_in.sem, mix_in.at(i, b + 1))
                act.wait_ge(done.sem, done.at(i, b - 1))
                nc.scalar.activation(hi[:, b], mix[:], ACT.Copy).then_inc(hi_ready.sem, 1)

            def statistics(i, b):
                act.wait_ge(done.sem, done.at(i, b + 1))
                act.wait_ge(sums_ready.sem, sums_ready.at(i, b - 1))
                for h in range(2):
                    act.wait_ge(squared.sem, squared.at(i, 2 * b + h))
                    nc.scalar.activation(junk[:], ACC[b][h][:, :], ACT.Square,
                                         accum_out=sq[:, b, h:h + 1]).then_inc(squared.sem, 1)
                act.wait_ge(sums_ready.sem, sums_ready.at(i, b + 1))
                act.wait_ge(rstd_done.sem, rstd_done.at(i, b - 1))
                nc.scalar.activation(ln[:, b:b + 1], both[:, b:b + 1], ACT.Ln, scale=1.0 / DM,
                                     bias=k.eps[:]).then_inc(ln_done.sem, 1)
                act.wait_ge(ln_done.sem, ln_done.at(i, b + 1))
                act.wait_ge(added.sem, added.at(i, 2 * b - 2))
                nc.scalar.activation(rstd[:, b:b + 1], ln[:, b:b + 1], ACT.Exp, scale=-0.5).then_inc(rstd_done.sem, 1)

            split_mix(0, 0)
            for n in range(NW):
                act.wait_ge(w_in, 16 * (n + 1))
                nc.scalar.activation(w_hi[:, WC * n:WC * n + WC, :], raw[:], ACT.Copy).then_inc(w_hi_ready, 1)
                if n == 0:
                    split_mix(0, 1)
            for h in range(2):
                act.wait_ge(new_folded, h + 1)
                if h:
                    act.wait_ge(new_act, 1)
                nc.scalar.activation(new_tmp[:], FOLDED[h][0:NB, :], ACT.Square, accum_out=new_sq[:, h:h + 1]).then_inc(new_act, 1)
            act.wait_ge(new_step, 3)
            nc.scalar.activation(new_stat[:, 1:2], new_stat[:, 0:1], ACT.Ln, scale=1.0 / DM, bias=k.eps[0:NB, :]).then_inc(new_act, 1)
            act.wait_ge(new_act, 3)
            nc.scalar.activation(new_stat[:, 2:3], new_stat[:, 1:2], ACT.Exp, scale=-0.5).then_inc(new_act, 1)
            with act.Fori(0, TB // 2 - 1) as i:
                for b in range(2):
                    statistics(i, b)
                    split_mix(i + 1, b)
            for b in range(2):
                statistics(TB // 2 - 1, b)

        @block.vector
        def _(dve):
            for s in (lo_ready, sums_ready, scaled, added):
                s.credit(dve)
            for h in range(2):
                nc.vector.memset(NEW[h][:, :], 0.0).then_inc(cleared, 1)

            def split_mix(i, b):
                dve.wait_ge(hi_ready.sem, hi_ready.at(i, b + 1))
                nc.vector.tensor_tensor(lo[:, b], mix[:], hi[:, b].bitcast(F32), ALU.subtract).then_inc(lo_ready.sem, 1)

            def normed_rows(i, b):
                dve.wait_ge(squared.sem, squared.at(i, 2 * b + 2))
                dve.wait_ge(ln_done.sem, ln_done.at(i, b - 1))
                nc.vector.tensor_tensor(both[:, b:b + 1], sq[:, b, 0:1], sq[:, b, 1:2], ALU.add).then_inc(sums_ready.sem, 1)
                dve.wait_ge(rstd_done.sem, rstd_done.at(i, b + 1))
                dve.wait_ge(x_in[b].sem, x_in[b].at(i, 1))
                for h in range(2):
                    cs = slice(h * H, (h + 1) * H)
                    dve.wait_ge(added.sem, added.at(i, 2 * b + h))
                    nc.vector.scalar_tensor_tensor(out=tmp[:], in0=ACC[b][h][:, :], scalar=rstd[:, b:b + 1],
                                                   in1=gain[:, cs], op0=ALU.mult, op1=ALU.mult).then_inc(scaled.sem, 1)
                    dve.wait_ge(scaled.sem, scaled.at(i, 2 * b + h + 1))
                    nc.vector.tensor_tensor(x[:, b, cs], x[:, b, cs], tmp[:], ALU.add).then_inc(added.sem, 1)

            split_mix(0, 0)
            for n in range(NW):
                dve.wait_ge(w_hi_ready, n + 1)
                nc.vector.tensor_tensor(w_lo[:, WC * n:WC * n + WC, :], raw[:], w_hi[:, WC * n:WC * n + WC, :].bitcast(F32),
                                        ALU.subtract).then_inc(w_lo_ready, 1)
                if n == 0:
                    split_mix(0, 1)
            dve.wait_ge(new_added, NW)
            for h in range(2):
                if h:
                    dve.wait_ge(new_folded, 1)
                nc.vector.tensor_copy(new_rows[:], NEW[h][:, :]).then_inc(new_step, 1)
            dve.wait_ge(new_act, 2)
            nc.vector.tensor_tensor(new_stat[:, 0:1], new_sq[:, 0:1], new_sq[:, 1:2], ALU.add).then_inc(new_step, 1)
            dve.wait_ge(new_act, 4)
            dve.wait_ge(new_x_in, 16)
            dve.wait_ge(gain_in, 16)
            for h in range(2):
                cs = slice(h * H, (h + 1) * H)
                dve.wait_ge(new_step, 3 + 2 * h)
                nc.vector.scalar_tensor_tensor(out=new_tmp[:], in0=FOLDED[h][0:NB, :], scalar=new_stat[:, 2:3],
                                               in1=gain[0:NB, cs], op0=ALU.mult, op1=ALU.mult).then_inc(new_step, 1)
                dve.wait_ge(new_step, 4 + 2 * h)
                nc.vector.tensor_tensor(new_x[:, cs], new_x[:, cs], new_tmp[:], ALU.add).then_inc(new_step, 1)
            with dve.Fori(0, TB // 2 - 1) as i:
                for b in range(2):
                    normed_rows(i, b)
                    split_mix(i + 1, b)
            for b in range(2):
                normed_rows(TB // 2 - 1, b)

        @block.tensor
        def _(pe):
            done.credit(pe)

            def products(b, kk):
                for h in range(2):
                    for n, (m, w) in enumerate(((hi, w_hi), (hi, w_lo), (lo, w_hi))):
                        last = nc.tensor.matmul(ACC[b][h][:, :], m[:, b, kk, :], w[:, kk, h * H:(h + 1) * H],
                                                start=(kk == 0 and n == 0), stop=(kk == KO - 1 and n == 2))
                return last

            pe.wait_ge(cleared, 2)
            pe.wait_ge(hi_ready.sem, hi_ready.at(0, 1))
            pe.wait_ge(lo_ready.sem, lo_ready.at(0, 1))
            for c in range(NW):
                pe.wait_ge(w_in, 16 * (c + 1))
                for e in range(WC):
                    kk = WC * c + e
                    for h in range(2):
                        g = 32 * ((2 * e + c) % 4)
                        last = nc.tensor.matmul(NEW[h][g:g + NB, :], k.new_mix[:, kk, :], raw[:, e, h * H:(h + 1) * H],
                                                start=(c < 2), stop=(c >= NW - 2), skip_group_check=True)
                last.then_inc(new_added, 1)
                pe.wait_ge(w_hi_ready, c + 1)
                pe.wait_ge(w_lo_ready, c + 1)
                if c == 1:
                    pe.wait_ge(hi_ready.sem, hi_ready.at(0, 2))
                    pe.wait_ge(lo_ready.sem, lo_ready.at(0, 2))
                for b in range(2):
                    if b == 1 and c == 0:
                        continue
                    for kk in range(0 if b == 1 and c == 1 else WC * c, WC * c + WC):
                        last = products(b, kk)
                    if c == NW - 1:
                        last.then_inc(done.sem, 1)
            for h in range(2):
                pe.wait_ge(new_step, h + 1)
                nc.tensor.matmul(FOLDED[h][0:NB, :], k.fold[:], new_rows[:], start=True, stop=True).then_inc(new_folded, 1)
            with pe.Fori(1, TB // 2) as i:
                for b in range(2):
                    pe.wait_ge(added.sem, added.at(i, 2 * b - 2))
                    pe.wait_ge(hi_ready.sem, hi_ready.at(i, b + 1))
                    pe.wait_ge(lo_ready.sem, lo_ready.at(i, b + 1))
                    for kk in range(KO):
                        last = products(b, kk)
                    last.then_inc(done.sem, 1)


OUTS = (("y_prompt", (1, T, DM)), ("y_sample", (NB, 1, DM)),
        ("pool_prompt", (1, 1, POOL_BUF, GW)), ("pool_sample", (1, NB, POOL_BUF, GW)),
        ("C_prompt", (1, 1, MLH, DK, DK)), ("C_sample", (1, NB, MLH, DK, DK)),
        ("n_prompt", (1, 1, MLH, DK)), ("n_sample", (1, NB, MLH, DK)),
        ("m_prompt", (1, 1, MLH)), ("m_sample", (1, NB, MLH)),
        ("k_prompt", (1, 1, T, SBH, SBD)), ("k_sample", (1, NB, 1, SBH, SBD)),
        ("v_prompt", (1, 1, T, SBH, SBD)), ("v_sample", (1, NB, 1, SBH, SBD)),
        ("mem_k", (1, 1, NMEM, MLH, DK)), ("mem_v", (1, 1, NMEM, MLH, DK)))


class Operands:

    def __init__(self, nc, ins, outs):
        self.norm_pre, self.norm_post, self.mem_norm = ins["norm_pre"], ins["norm_post"], ins["mem_norm"]
        self.mem_prompt, self.page_table, self.sb_logit_bias = ins["mem_prompt"], ins["page_table"], ins["sb_logit_bias"]
        self.x_prompt = ins["x_prompt"].rearrange("a (r p) d -> (a r) p d", p=P)
        self.x_by_block = ins["x_prompt"].rearrange("a (r p) d -> p (a r) d", p=P)
        self.x_sample = ins["x_sample"].rearrange("b t d -> (b t) d")
        self.w_in, self.w_mem, self.w_out = (ins[n].rearrange("o (k p) c -> p (o k) c", p=P)
                                             for n in ("w_in", "w_mem_kv", "w_out"))
        self.state_pool = ins["state_pool_buf"].rearrange("o b r c -> (o b) r c")
        self.pool_scale = ins["pool_scale"].rearrange("o (g c) -> c (o g)", c=P)
        self.pool_w = ins["pool_w"].rearrange("o g c d -> c (o g) d")
        self.gate_bias = ins["mlstm_gate_bias"].rearrange("o g h -> (g h) o")
        self.mlstm_norm = ins["mlstm_norm"].rearrange("o (h d) -> d (o h)", d=P)
        self.state_m = ins["state_mlstm_m"].rearrange("o b h -> (o b) h")
        self.state_n = ins["state_mlstm_n"].rearrange("o b h n -> (o b h) n")
        self.state_C = ins["state_mlstm_C"].rearrange("o b h k v -> k (o b) h v")
        scratch = lambda name, shape: nc.dram_tensor(name, shape, F32, kind="Internal").ap()
        self.gates_dram, self.new_gates_dram = scratch("gates", [2 * MLH, T]), scratch("new_gates", [2 * MLH, NB])
        self.rows_dram, self.new_rows_dram = scratch("gate_rows", [3, MLH, T]), scratch("new_gate_rows", [NB, 3 * MLH])
        self.q_dram = scratch("new_q", [NB, GW])
        self.n_phys = ins["cache_sb_k"].shape[1]
        self.cache_k, self.cache_v = (ins[n].rearrange("o n s h d -> (o n s) (h d)") for n in ("cache_sb_k", "cache_sb_v"))
        self.mix_dram = scratch("mix", [4 * GT, P, T])
        self.cache_mem_k, self.cache_mem_v = (ins[n].rearrange("o b (m p) h d -> p (o b m) (h d)", p=P)
                                              for n in ("cache_mem_k", "cache_mem_v"))

        self.y_by_block = outs["y_prompt"].rearrange("a (r p) d -> p (a r) d", p=P)
        self.y_sample = outs["y_sample"].rearrange("b t d -> (b t) d")
        self.pool_prompt = outs["pool_prompt"].rearrange("a b r c -> (a b r) c")
        self.pool_sample = outs["pool_sample"].rearrange("a b r c -> (a b) r c")
        self.C_prompt = outs["C_prompt"].rearrange("a b h k v -> k (a b h) v")
        self.C_sample = outs["C_sample"].rearrange("a b h k v -> k (a b) h v")
        self.n_prompt, self.n_sample = (outs[n].rearrange("a b h k -> (a b) (h k)") for n in ("n_prompt", "n_sample"))
        self.m_prompt, self.m_sample = (outs[n].rearrange("a b h -> (a b) h") for n in ("m_prompt", "m_sample"))
        self.sb_k_prompt, self.sb_v_prompt = (outs[n].rearrange("a b (j p) h d -> p (a b j) (h d)", p=P)
                                              for n in ("k_prompt", "v_prompt"))
        self.sb_k_sample, self.sb_v_sample = (outs[n].rearrange("a b t h d -> (a b t) (h d)")
                                              for n in ("k_sample", "v_sample"))
        self.mem_k, self.mem_v = (outs[n].rearrange("a b (m p) h d -> p (a b m) (h d)", p=P) for n in ("mem_k", "mem_v"))


def build(nc, ins, outs):
    k = Operands(nc, ins, outs)
    with ExitStack() as ctx:
        sb = lambda name, shape, dt=F32: ctx.enter_context(nc.sbuf_tensor(name, shape, dt))
        k.bank = [ctx.enter_context(nc.psum_tensor(f"bank{n}", [P, 512], F32)) for n in range(8)]
        with stage(nc):
            constants(nc, ctx, k)
        k.new_mix = sb("new_mix", [P, 4 * GT, NB])
        k.y_new = sb("y_new", [P, GT, NB])
        normed = ctx.enter_context(ExitStack())
        k.xh, k.xl = (normed.enter_context(nc.sbuf_tensor(name, [P, KT, NT], F32R)) for name in ("xh", "xl"))
        quads = [bank[:, :].rearrange("p (b t) -> p b t", b=4) for bank in k.bank]
        rows = [(k.x_prompt[r], P, r * P) for r in range(TB)] + [(k.x_sample, NB, T)]
        with stage(nc) as inner:
            normalise_and_transpose(nc, inner, "n", rows, k.norm_pre, k.xh, k.xl, k.ident, k.eps, quads)
        with stage(nc) as inner:
            new_queries(nc, inner, k)
        with stage(nc) as inner:
            stick_breaking_prompt(nc, inner, k)
        with stage(nc) as inner:
            stick_breaking_new(nc, inner, k)
        with ExitStack() as gates:
            k.a_col = gates.enter_context(nc.sbuf_tensor("a_col", [P, MLH * TB], F32))
            k.n_old = gates.enter_context(nc.sbuf_tensor("n_old", [P, MLH, NB], F32))
            with stage(nc) as inner:
                mlstm_gates(nc, inner, k)
            with stage(nc) as inner:
                mlstm(nc, inner, k)
        with ExitStack() as memory:
            k.mem_kT = memory.enter_context(nc.sbuf_tensor("mem_kT", [P, MLH, NMEM], F32))
            k.mem_v_tok = memory.enter_context(nc.sbuf_tensor("mem_v_tok", [P, MLH, NMEM // P, P], F32))
            with stage(nc) as inner:
                memory_keys(nc, inner, k)
            with stage(nc) as inner:
                memory_and_pooling(nc, inner, k)
        normed.close()
        with stage(nc) as inner:
            output(nc, inner, k)


def kernel(**inputs):
    import numpy as np
    import concourse.bacc as bacc
    from concourse.bass_utils import run_bass_kernel_spmd

    nc = bacc.Bacc("TRN2", target_bir_lowering=False, num_devices=1)
    arrays = {name: np.ascontiguousarray(a) for name, a in inputs.items()}
    ins = {name: nc.dram_tensor(name, a.shape, mybir.dt.from_np(a.dtype), kind="ExternalInput").ap()
           for name, a in arrays.items()}
    outs = {name: nc.dram_tensor("out_" + name, shape, F32, kind="ExternalOutput").ap() for name, shape in OUTS}
    build(nc, ins, outs)
    result = run_bass_kernel_spmd(nc, [arrays], core_ids=[0]).results[0]
    return tuple(result["out_" + name] for name, _ in OUTS)
```
